# Optimizing a Trainium2 kernel written in Bass

```python
import jax, jax.numpy as jnp
from jax import lax
import numpy as np

D_MODEL = 1024
BATCH = 1
SEQ = 2048
DEPTH = 2

GRID_W = 64
CTX_LEN = 256
HEAD_DIM = 64
N_Q_HEADS = 12
N_KV_HEADS = 4
Q_PER_KV = N_Q_HEADS // N_KV_HEADS
ATTN_W = N_Q_HEADS * HEAD_DIM
KV_W = N_KV_HEADS * HEAD_DIM
ROPE_THETA = 10000.0
ROPE_PAIRS = HEAD_DIM // 4
Q_BLOCK = 128
N_FGROUPS = 4
FGROUP_W = 64
FNET_W = N_FGROUPS * FGROUP_W
EVEN_MIX_W = ATTN_W + FNET_W
EVEN_IN_W = 2 * ATTN_W + 2 * KV_W + 2 * FNET_W
EVEN_SPLITS = [ATTN_W, 2 * ATTN_W, 2 * ATTN_W + KV_W, 2 * ATTN_W + 2 * KV_W, 2 * ATTN_W + 2 * KV_W + FNET_W]
MLSTM_HEADS = 4
MLSTM_HEAD_DIM = 256
MLSTM_W = MLSTM_HEADS * MLSTM_HEAD_DIM
CHUNK = 128
N_GATES = 4 * MLSTM_HEADS
ODD_IN_W = 5 * MLSTM_W + N_GATES
ODD_SPLITS = [MLSTM_W, 2 * MLSTM_W, 3 * MLSTM_W, 4 * MLSTM_W, 5 * MLSTM_W]

N_EVEN = (DEPTH + 1) // 2
N_ODD = DEPTH // 2
ALPHA = (2.0 * DEPTH) ** 0.25
BETA = (8.0 * DEPTH) ** -0.25
EPS = 1e-6

kernel_name = 'hybrid_gqa_fnet_mlstm_prefix_dit'

def layer_norm(x):
    xf = x.astype(jnp.float32)
    mu = jnp.mean(xf, -1, keepdims=True)
    var = jnp.mean(jnp.square(xf - mu), -1, keepdims=True)
    return ((xf - mu) * lax.rsqrt(var + EPS)).astype(x.dtype)

def rms_norm(x, gain):
    xf = x.astype(jnp.float32)
    y = xf * lax.rsqrt(jnp.mean(jnp.square(xf), -1, keepdims=True) + EPS)
    return (y * gain.astype(jnp.float32)).astype(x.dtype)

def axial_rope_tables(n_tokens):
    rows = n_tokens // GRID_W
    row_idx = jnp.repeat(jnp.arange(rows, dtype=jnp.float32), GRID_W)
    col_idx = jnp.tile(jnp.arange(GRID_W, dtype=jnp.float32), rows)
    inv_freq = jnp.power(ROPE_THETA, -jnp.arange(ROPE_PAIRS, dtype=jnp.float32) / ROPE_PAIRS)
    ang = jnp.concatenate([row_idx[:, None] * inv_freq, col_idx[:, None] * inv_freq], axis=-1)
    return jnp.cos(ang), jnp.sin(ang)

def apply_rope(x, cos, sin):
    xf = x.astype(jnp.float32)
    half = HEAD_DIM // 2
    x1, x2 = xf[..., :half], xf[..., half:]
    cs, sn = cos[None, :, None, :], sin[None, :, None, :]
    return jnp.concatenate([x1 * cs - x2 * sn, x1 * sn + x2 * cs], axis=-1).astype(x.dtype)

def attend(q, k, v):
    s = jnp.einsum('bqhgd,bkhd->bhgqk', q, k, preferred_element_type=jnp.float32) * (HEAD_DIM ** -0.5)
    p = jax.nn.softmax(s, axis=-1).astype(v.dtype)
    return jnp.einsum('bhgqk,bkhd->bqhgd', p, v)

def blocked_attention(q, k, v):
    b, t = q.shape[:2]
    nb = t // Q_BLOCK
    qb = q.reshape(b, nb, Q_BLOCK, N_KV_HEADS, Q_PER_KV, HEAD_DIM).transpose(1, 0, 2, 3, 4, 5)
    o = lax.map(lambda qi: attend(qi, k, v), qb)
    return o.transpose(1, 0, 2, 3, 4, 5).reshape(b, t, ATTN_W)

def fourier_mix(u, gain, w_mix):
    un = rms_norm(u, gain).astype(jnp.float32)
    f = jnp.fft.fft2(un, axes=(1, 3), norm='ortho').real.astype(u.dtype)
    return jnp.einsum('btgc,gcd->btgd', f, w_mix)

def mlstm_scan(q, k, v, log_i, log_f, state):
    b, t, h, d = q.shape
    nc = t // CHUNK
    to_chunks = lambda a: a.reshape(b, nc, CHUNK, h, d).transpose(1, 0, 3, 2, 4)
    g_chunks = lambda a: a.reshape(b, nc, CHUNK, h).transpose(1, 0, 3, 2)
    mask = jnp.tril(jnp.ones((CHUNK, CHUNK), dtype=bool))

    def step(carry, inp):
        c_mat, n_vec, m = carry
        qc, kc, vc, li, lf = inp
        cum = jnp.cumsum(lf, axis=-1)
        d_log = jnp.where(mask, cum[..., :, None] - cum[..., None, :] + li[..., None, :], -jnp.inf)
        inter = cum + m[..., None]
        m_t = jnp.maximum(inter, jnp.max(d_log, axis=-1))
        d_w = jnp.exp(d_log - m_t[..., None])
        inter_w = jnp.exp(inter - m_t)
        s = jnp.einsum('bhtd,bhsd->bhts', qc, kc) * d_w
        num = jnp.einsum('bhts,bhse->bhte', s, vc) + inter_w[..., None] * jnp.einsum('bhtd,bhde->bhte', qc, c_mat)
        den = jnp.sum(s, axis=-1) + inter_w * jnp.einsum('bhtd,bhd->bht', qc, n_vec)
        out = num / jnp.maximum(jnp.abs(den), jnp.exp(-m_t))[..., None]
        tot = cum[..., -1]
        w_log = tot[..., None] - cum + li
        m_new = jnp.maximum(tot + m, jnp.max(w_log, axis=-1))
        w = jnp.exp(w_log - m_new[..., None])
        decay = jnp.exp(tot + m - m_new)
        kw = kc * w[..., None]
        c_new = decay[..., None, None] * c_mat + jnp.einsum('bhsd,bhse->bhde', kw, vc)
        n_new = decay[..., None] * n_vec + jnp.sum(kw, axis=2)
        return (c_new, n_new, m_new), out

    state, outs = lax.scan(step, state, (to_chunks(q), to_chunks(k), to_chunks(v), g_chunks(log_i), g_chunks(log_f)))
    return outs.transpose(1, 0, 3, 2, 4).reshape(b, t, h, d), state

def zero_state(b):
    return (jnp.zeros((b, MLSTM_HEADS, MLSTM_HEAD_DIM, MLSTM_HEAD_DIM), jnp.float32),
            jnp.zeros((b, MLSTM_HEADS, MLSTM_HEAD_DIM), jnp.float32),
            jnp.zeros((b, MLSTM_HEADS), jnp.float32))

def bidir_mlstm(q, k, v, gates, state_f, state_b):
    li_f, lf_f, li_b, lf_b = gates
    flip = lambda a: jnp.flip(a, axis=1)
    h_f, end_f = mlstm_scan(q, k, v, li_f, lf_f, state_f)
    h_b, end_b = mlstm_scan(flip(q), flip(k), flip(v), flip(li_b), flip(lf_b), state_b)
    return h_f + flip(h_b), end_f, end_b

def even_mixer(h_lat, h_ctx, w_in, q_gain, k_gain, f_gain, w_fmix, w_out, cos, sin, need_ctx):
    def project(h):
        b, t = h.shape[:2]
        q, ga, k, v, u, gb = jnp.split(h @ w_in, EVEN_SPLITS, axis=-1)
        q = rms_norm(q.reshape(b, t, N_Q_HEADS, HEAD_DIM), q_gain)
        k = rms_norm(k.reshape(b, t, N_KV_HEADS, HEAD_DIM), k_gain)
        return q, ga, k, v.reshape(b, t, N_KV_HEADS, HEAD_DIM), u.reshape(b, t, N_FGROUPS, FGROUP_W), gb

    def merge(a, ga, f, gb):
        b, t = ga.shape[:2]
        y = jnp.concatenate([a * jax.nn.silu(ga), f.reshape(b, t, FNET_W) * jax.nn.silu(gb)], axis=-1)
        return y @ w_out

    qc, gac, kc, vc, uc, gbc = project(h_ctx)
    ql, gal, kl, vl, ul, gbl = project(h_lat)
    ql = apply_rope(ql, cos, sin)
    kl = apply_rope(kl, cos, sin)
    k_all = jnp.concatenate([kc, kl], axis=1)
    v_all = jnp.concatenate([vc, vl], axis=1)
    y_lat = merge(blocked_attention(ql, k_all, v_all), gal, fourier_mix(ul, f_gain, w_fmix), gbl)
    y_ctx = None
    if need_ctx:
        b, t = qc.shape[:2]
        a_ctx = attend(qc.reshape(b, t, N_KV_HEADS, Q_PER_KV, HEAD_DIM), kc, vc).reshape(b, t, ATTN_W)
        y_ctx = merge(a_ctx, gac, fourier_mix(uc, f_gain, w_fmix), gbc)
    return y_lat, y_ctx

def odd_mixer(h_lat, h_ctx, w_in, gate_bias, w_out, need_ctx):
    def project(h):
        b, t = h.shape[:2]
        q, k, v, o, z, g = jnp.split(h @ w_in, ODD_SPLITS, axis=-1)
        heads = lambda a: a.astype(jnp.float32).reshape(b, t, MLSTM_HEADS, MLSTM_HEAD_DIM)
        g = (g.astype(jnp.float32) + gate_bias.astype(jnp.float32)).reshape(b, t, 4, MLSTM_HEADS)
        gates = (g[:, :, 0], jax.nn.log_sigmoid(g[:, :, 1]), g[:, :, 2], jax.nn.log_sigmoid(g[:, :, 3]))
        return heads(q), heads(k) * (MLSTM_HEAD_DIM ** -0.5), heads(v), o, z, gates

    def merge(hsum, o, z):
        b, t = o.shape[:2]
        y = jax.nn.sigmoid(o) * hsum.reshape(b, t, MLSTM_W).astype(o.dtype) * jax.nn.silu(z)
        return y @ w_out

    b = h_lat.shape[0]
    qc, kc, vc, oc, zc, gc = project(h_ctx)
    hc, end_f, end_b = bidir_mlstm(qc, kc, vc, gc, zero_state(b), zero_state(b))
    ql, kl, vl, ol, zl, gl = project(h_lat)
    hl, _, _ = bidir_mlstm(ql, kl, vl, gl, end_f, end_b)
    y_lat = merge(hl, ol, zl)
    y_ctx = merge(hc, oc, zc) if need_ctx else None
    return y_lat, y_ctx

def setup_inputs(seed: int = 0) -> dict:
    key = jax.random.key(seed)
    ks = jax.random.split(key, 17)
    nrm = lambda k, shape, std: jax.random.normal(k, shape, jnp.float32) * std
    lin = jnp.linspace(3.0, 6.0, MLSTM_HEADS, dtype=jnp.float32)
    zer = jnp.zeros((MLSTM_HEADS,), jnp.float32)
    gate_base = jnp.concatenate([zer, lin, zer, lin])
    return {
        'x': nrm(ks[0], (BATCH, SEQ, D_MODEL), 1.0),
        'c': nrm(ks[1], (BATCH, D_MODEL), 1.0),
        'ctx': nrm(ks[2], (BATCH, CTX_LEN, D_MODEL), 1.0),
        'c_ctx': nrm(ks[3], (D_MODEL,), 1.0),
        'ada_w': nrm(ks[4], (DEPTH, D_MODEL, 3 * D_MODEL), 0.5 * D_MODEL ** -0.5),
        'ada_b': nrm(ks[5], (DEPTH, 3 * D_MODEL), 0.02),
        'post_ln_gain': 1.0 + nrm(ks[6], (DEPTH, D_MODEL), 0.02),
        'post_ln_bias': nrm(ks[7], (DEPTH, D_MODEL), 0.02),
        'even_w_in': nrm(ks[8], (N_EVEN, D_MODEL, EVEN_IN_W), D_MODEL ** -0.5),
        'even_q_gain': 1.0 + nrm(ks[9], (N_EVEN, HEAD_DIM), 0.02),
        'even_k_gain': 1.0 + nrm(ks[10], (N_EVEN, HEAD_DIM), 0.02),
        'even_f_gain': 1.0 + nrm(ks[11], (N_EVEN, N_FGROUPS, FGROUP_W), 0.02),
        'even_w_fmix': nrm(ks[12], (N_EVEN, N_FGROUPS, FGROUP_W, FGROUP_W), FGROUP_W ** -0.5),
        'even_w_out': nrm(ks[13], (N_EVEN, EVEN_MIX_W, D_MODEL), BETA * EVEN_MIX_W ** -0.5),
        'odd_w_in': nrm(ks[14], (N_ODD, D_MODEL, ODD_IN_W), D_MODEL ** -0.5),
        'odd_gate_bias': gate_base + nrm(ks[15], (N_ODD, N_GATES), 0.1),
        'odd_w_out': nrm(ks[16], (N_ODD, MLSTM_W, D_MODEL), BETA * MLSTM_W ** -0.5),
    }

def reference(x, c, ctx, c_ctx, ada_w, ada_b, post_ln_gain, post_ln_bias,
              even_w_in, even_q_gain, even_k_gain, even_f_gain, even_w_fmix, even_w_out,
              odd_w_in, odd_gate_bias, odd_w_out):
    n_tokens = x.shape[1]
    cos, sin = axial_rope_tables(n_tokens)
    silu_c = jax.nn.silu(c)
    silu_cc = jax.nn.silu(c_ctx)
    for i in range(DEPTH):
        last = i == DEPTH - 1
        sh_l, sc_l, g_l = jnp.split(silu_c @ ada_w[i] + ada_b[i], 3, axis=-1)
        sh_c, sc_c, g_c = jnp.split(silu_cc @ ada_w[i] + ada_b[i], 3, axis=-1)
        h_lat = layer_norm(x) * (1.0 + sc_l[:, None, :]) + sh_l[:, None, :]
        h_ctx = layer_norm(ctx) * (1.0 + sc_c) + sh_c
        if i % 2 == 0:
            j = i // 2
            y_lat, y_ctx = even_mixer(h_lat, h_ctx, even_w_in[j], even_q_gain[j], even_k_gain[j],
                                      even_f_gain[j], even_w_fmix[j], even_w_out[j], cos, sin, not last)
        else:
            j = i // 2
            y_lat, y_ctx = odd_mixer(h_lat, h_ctx, odd_w_in[j], odd_gate_bias[j], odd_w_out[j], not last)
        x = layer_norm(ALPHA * x + g_l[:, None, :] * y_lat) * post_ln_gain[i] + post_ln_bias[i]
        if not last:
            ctx = layer_norm(ALPHA * ctx + g_c * y_ctx) * post_ln_gain[i] + post_ln_bias[i]
    return x


_drawn_inputs = setup_inputs


def setup_inputs(seed=0):
    import zlib

    import numpy as np

    out = dict(_drawn_inputs(seed))
    spreads = {}
    factors = {'even_q_gain': 8.0, 'even_k_gain': 8.0, 'even_f_gain': 21.807}
    for name, (base, spread) in spreads.items():
        noise = np.random.default_rng([zlib.crc32(name.encode()), seed]).standard_normal(out[name].shape)
        drawn = base * np.exp(spread * noise) if base else spread * noise
        out[name] = __import__('jax').numpy.asarray(drawn.astype(out[name].dtype))
    for name, factor in factors.items():
        out[name] = (out[name] * factor).astype(out[name].dtype)
    return out
```

```python
from contextlib import ExitStack

import numpy as np

import concourse.bass as bass
from concourse import mybir

F32 = mybir.dt.float32
F32R = mybir.dt.float32r
ALU = mybir.AluOpType
ACT = mybir.ActivationFunctionType
AX = mybir.AxisListType

P = 128
D = 1024
KD = D // P
SEQ, CTX = 2048, 256
T = SEQ + CTX
NT = T // P
CT = CTX // P
LT = SEQ // P
GRID_W = 64
HD = 64
NQ, NKV = 12, 4
QPK = NQ // NKV
QW, KVW, FW = NQ * HD, NKV * HD, 256
MH, MD = 4, 256
W0_COLS = 2560
W1_COLS = 5 * D
CH = 512
EPS = 1e-6
ALPHA = 4.0 ** 0.25
MASKED = 1e30
C_QK, C_V, C_U, C_GATE = 0, QW + KVW, QW + 2 * KVW, QW + 2 * KVW + FW
C1_K, C1_V, C1_Q, C1_O, C1_Z = (i * D for i in range(5))
NR = 36
DIR_ROW = (0, 32)
PARTS = ((0, 10), (10, 8))


class Memory:

    def __init__(self, nc):
        self.nc, self.stack, self.all, self.sems = nc, ExitStack(), ExitStack(), []

    def sb(self, name, shape, dt=F32):
        return self.stack.enter_context(self.nc.sbuf_tensor(name, shape, dt))

    def ps(self, name, shape=(P, 512)):
        return self.stack.enter_context(self.nc.psum_tensor(name, list(shape), F32))

    def sem(self, name, count=None):
        new = [self.nc.alloc_semaphore(name if count is None else f"{name}{i}") for i in range(count or 1)]
        self.sems += new
        return new[0] if count is None else new

    def free(self):
        self.stack.close()
        self.stack = ExitStack()

    def end(self):
        self.stack.close()
        self.stack = ExitStack()
        if self.sems:
            self.nc.all_engine_barrier()
            self.nc.clear_and_free_semaphores(self.sems)
            self.nc.all_engine_barrier()
            self.sems = []


class Steps:

    def __init__(self, eng, sem, base=0):
        self.eng, self.sem, self.base, self.n = eng, sem, base, 0

    def did(self, ins):
        ins.then_inc(self.sem, 1)
        self.n += 1

    def wait(self):
        self.eng.wait_ge(self.sem, self.base + self.n)


def modulation(nc, m, a, s, keep):
    ct = m.sb("mod_c", [P, KD, 2])
    sil = m.sb("mod_silu", [P, KD, 2])
    sil_row = m.sb("mod_silu_row", [P, 2, KD, P])
    wbuf = m.sb("mod_w", [P, 2, KD, CH])
    bcol = m.sb("mod_bcol", [P, 2, 16])
    brow = m.sb("mod_brow", [P, 2, D])
    cols = m.sb("mod_cols", [P, 2, 16, 2])
    gate = m.sb("mod_gate", [P, 6, CH])
    pcol = m.ps("mod_pcol")
    prow = [m.ps(f"mod_prow{i}") for i in range(2)]
    small = m.sem("mod_small")
    silu_done, rows_done = m.sem("mod_silu_done"), m.sem("mod_rows_done")
    w_ld = m.sem("mod_w_ld", 2)
    col_mm, col_done = m.sem("mod_col_mm"), m.sem("mod_col_done")
    row_mm, row_done = m.sem("mod_row_mm"), m.sem("mod_row_done")
    st = m.sem("mod_store")
    NCH = 6
    rows = [(l, src, h) for l in range(2) for h in range(2) for src in range(2) if (l, src) != (1, 1)]
    used, n_col, n_row = [], 0, 0
    for n in range(2 * NCH):
        if n % NCH < 4:
            n_col += 1
            used.append((col_mm, n_col))
        else:
            n_row += 2 if n < NCH else 1
            used.append((row_mm, n_row))
    PER_LAYER = 6
    with nc.Block() as block:

        @block.sync
        def _(sp):
            sp.dma_start(ct[:], a["c_cols"]).then_inc(small, 16)
            sp.dma_start(bcol[:], a["ada_b_cols"]).then_inc(small, 16)
            for l in range(2):
                sp.dma_start(brow[:, l, :], a["ada_b"][l:l + 1, 2 * D:3 * D].broadcast_to([P, D])).then_inc(small, 16)
            for n in range(2 * NCH):
                l, c = n // NCH, n % NCH
                if n >= 2:
                    sp.wait_ge(*used[n - 2])
                sp.dma_start(wbuf[:, n % 2], a["ada_w"][l, :, c * CH:(c + 1) * CH].rearrange("(k p) n -> p k n", p=P)).then_inc(w_ld[n % 2], 16)

        @block.scalar
        def _(act):
            act.wait_ge(small, 64)
            nc.scalar.activation(sil[:], ct[:], ACT.Silu).then_inc(silu_done, 1)
            for n, (l, src, h) in enumerate(rows):
                act.wait_ge(row_done, n + 1)
                act.dma_start(s["gates"][l * 2 + src, :, h * CH:(h + 1) * CH], gate[:, n, :]).then_inc(st, 16)
            act.wait_ge(st, 16 * len(rows))

        @block.vector
        def _(dve):
            dve.wait_ge(silu_done, 1)
            for src in range(2):
                nc.vector.tensor_copy(sil_row[:, src], sil[:, :, src:src + 1].broadcast_to([P, KD, P])).then_inc(rows_done, 1)
            nr = 0
            for l in range(2):
                dve.wait_ge(*used[l * NCH + 3])
                nc.vector.tensor_tensor(cols[:, l], pcol[:, 0:32].rearrange("p (t s) -> p t s", s=2),
                                        bcol[:, l, :].unsqueeze(2).broadcast_to([P, 16, 2]), ALU.add).then_inc(col_done, 1)
                dve.wait_ge(col_done, PER_LAYER * l + 1)
                nc.vector.tensor_scalar(cols[:, l, 8:16], cols[:, l, 8:16], 1.0, None, ALU.add).then_inc(col_done, 1)
                dve.wait_ge(col_done, PER_LAYER * l + 2)
                for which in range(2):
                    v = cols[:, l, 8 * which:8 * which + 8, :]
                    nc.vector.tensor_copy(keep["mod"][:, l, which, CT:NT, :], v[:, :, 0].unsqueeze(1).broadcast_to([P, LT, KD])).then_inc(col_done, 1)
                    nc.vector.tensor_copy(keep["mod"][:, l, which, 0:CT, :], v[:, :, 1].unsqueeze(1).broadcast_to([P, CT, KD])).then_inc(col_done, 1)
                for h in range(2):
                    for src in range(2 - l):
                        dve.wait_ge(row_mm, nr + 1)
                        nc.vector.tensor_tensor(gate[:, nr, :], prow[nr % 2][:], brow[:, l, h * CH:(h + 1) * CH], ALU.add).then_inc(row_done, 1)
                        nr += 1

        @block.tensor
        def _(pe):
            pe.wait_ge(rows_done, 2)
            nr = 0
            for n in range(2 * NCH):
                l, c = n // NCH, n % NCH
                pe.wait_ge(w_ld[n % 2], 16 * (n // 2 + 1))
                if c < 4:
                    if l == 1 and c == 0:
                        pe.wait_ge(col_done, 1)
                    for j in range(4):
                        t = 4 * c + j
                        for k in range(KD):
                            mm = nc.tensor.matmul(pcol[:, 2 * t:2 * t + 2], wbuf[:, n % 2, k, j * P:(j + 1) * P], sil[:, k, :],
                                                  start=(k == 0), stop=(k == KD - 1))
                    mm.then_inc(col_mm, 1)
                else:
                    for src in range(2 - l):
                        if nr >= 2:
                            pe.wait_ge(row_done, nr - 1)
                        for k in range(KD):
                            mm = nc.tensor.matmul(prow[nr % 2][:], sil_row[:, src, k, :], wbuf[:, n % 2, k, :], start=(k == 0), stop=(k == KD - 1))
                        mm.then_inc(row_mm, 1)
                        nr += 1
    m.end()


def normalised(nc, m, layer, x_src, mod, h_hi, h_lo, first, count, ident):
    tag = f"ln{layer}{first}_"
    x = m.sb(tag + "x", [P, 2, D])
    xn = m.sb(tag + "xn", [P, 2, D])
    hf = m.sb(tag + "h", [P, 2, KD, P])
    stats = m.sb(tag + "stats", [P, 2, 2, 6])
    mv = m.sb(tag + "mv", [P, 2, 2])
    rstd = m.sb(tag + "rstd", [P, 2, 1])
    mcol = m.sb(tag + "mcol", [P, 2, 2, KD])
    half, eps = m.sb(tag + "half", [P, 1]), m.sb(tag + "eps", [P, 1])
    tp = [m.ps(tag + f"tp{i}", (P, 2, 512)) for i in range(2)]
    x_ld, x_used = m.sem(tag + "x_ld", 2), m.sem(tag + "x_used", 2)
    chain, var_done, rstd_done = m.sem(tag + "chain"), m.sem(tag + "var"), m.sem(tag + "rstd_done")
    tr_done, hf_done = m.sem(tag + "tr", 2), m.sem(tag + "hf", 2)
    hi_done, lo_done, ready = m.sem(tag + "hi", 2), m.sem(tag + "lo", 2), m.sem(tag + "ready")
    K = 3 + KD - 1
    with nc.Block() as block:

        @block.sync
        def _(sp):
            with sp.Fori(0, count // 2) as v:
                for p in range(2):
                    sp.wait_ge(x_used[p], v)
                    sp.dma_start(x[:, p, :], x_src[bass.ds((2 * v + p + first) * P, P), :]).then_inc(x_ld[p], 16)

        @block.vector
        def _(dve):
            with dve.Fori(0, count // 2) as v:
                for p in range(2):
                    base = (2 * v + p) * K
                    c = Steps(dve, chain, base)
                    dve.wait_ge(x_ld[p], 16 * v + 16)
                    for h in range(2):
                        c.did(nc.vector.bn_stats(stats[:, p, h, :], x[:, p, h * 512:(h + 1) * 512]))
                    c.wait()
                    c.did(nc.vector.tensor_copy(mcol[:, p], mod[:, layer, :, 2 * v + p + first, :]))
                    nc.vector.bn_aggr(mv[:, p, :], stats[:, p].rearrange("p a b -> p (a b)")).then_inc(var_done, 1)
                    dve.wait_ge(rstd_done, 2 * v + p + 1)
                    dve.wait_ge(tr_done[p], v)
                    nc.vector.tensor_scalar(xn[:, p, :], x[:, p, :], mv[:, p, 0:1], rstd[:, p, :], ALU.subtract, ALU.mult).then_inc(x_used[p], 1)
                    c.wait()
                    dve.wait_ge(tr_done[p], v + 1)
                    dve.wait_ge(lo_done[p], v)
                    for k in range(KD):
                        ins = nc.vector.tensor_scalar(hf[:, p, k, :], tp[p][:, k // 4, (k % 4) * P:(k % 4 + 1) * P],
                                                      mcol[:, p, 1, k:k + 1], mcol[:, p, 0, k:k + 1], ALU.mult, ALU.add)
                        if k < KD - 1:
                            c.did(ins)
                        else:
                            ins.then_inc(hf_done[p], 1)
                    assert c.n == K, c.n

        @block.gpsimd
        def _(pool):
            nc.gpsimd.memset(half[:], -0.5).then_inc(ready, 1)
            nc.gpsimd.memset(eps[:], EPS).then_inc(ready, 1)
            pool.wait_ge(ready, 2)
            with pool.Fori(0, count // 2) as v:
                for p in range(2):
                    n = 2 * v + p
                    pool.wait_ge(var_done, n + 1)
                    nc.gpsimd.tensor_tensor(rstd[:, p, :], mv[:, p, 1:2], eps[:], ALU.add).then_inc(ready, 1)
                    pool.wait_ge(ready, n + 3)
                    nc.gpsimd.tensor_tensor(rstd[:, p, :], rstd[:, p, :], half[:], ALU.pow).then_inc(rstd_done, 1)
                    pool.wait_ge(hi_done[p], v + 1)
                    nc.gpsimd.tensor_tensor(h_lo[:, :, n, :], hf[:, p], h_hi[:, :, n, :].bitcast(F32), ALU.subtract).then_inc(lo_done[p], 1)

        @block.scalar
        def _(act):
            with act.Fori(0, count // 2) as v:
                for p in range(2):
                    act.wait_ge(hf_done[p], v + 1)
                    nc.scalar.activation(h_hi[:, :, 2 * v + p, :], hf[:, p], ACT.Copy).then_inc(hi_done[p], 1)

        @block.tensor
        def _(pe):
            with pe.Fori(0, count // 2) as v:
                for p in range(2):
                    pe.wait_ge(x_used[p], v + 1)
                    pe.wait_ge(hf_done[p], v)
                    for k in range(KD):
                        tr = nc.tensor.transpose(tp[p][:, k // 4, (k % 4) * P:(k % 4 + 1) * P], xn[:, p, k * P:(k + 1) * P], ident[:])
                    tr.then_inc(tr_done[p], 1)


def split_mm(nc, out, s_hi, s_lo, m_hi, m_lo, start, stop):
    nc.tensor.matmul(out, s_hi, m_hi, start=start, stop=False)
    nc.tensor.matmul(out, s_hi, m_lo, start=False, stop=False)
    return nc.tensor.matmul(out, s_lo, m_hi, start=False, stop=stop)


def projected(nc, m, tag, w_src, out, h_hi, h_lo, wbuf, chunks, first, tiles, gates=None):
    wst, whi, wlo = wbuf
    nt = len(tiles)
    NS = nt // 2
    stage = m.sb(tag + "stage", [P, NS, CH])
    acc = [m.ps(tag + f"acc{i}") for i in range(NS)]
    w_ld, hi_done, lo_done = m.sem(tag + "w_ld"), m.sem(tag + "w_hi"), m.sem(tag + "w_lo")
    used = m.sem(tag + "w_used", 2)
    mm_done, out_done, stored = m.sem(tag + "mm", NS), m.sem(tag + "out", NS), m.sem(tag + "stored", NS)
    c0, nch = chunks[0], len(chunks)
    if gates is not None:
        wg, wg_hi, wg_lo, graw, gbias, wg_src, gbias_src = gates
        gacc = [m.ps(tag + f"gacc{i}") for i in range(2)]
        g_ld, g_split, g_mm, g_out = m.sem(tag + "g_ld"), m.sem(tag + "g_split"), m.sem(tag + "g_mm"), m.sem(tag + "g_out")
        spans = [(t0, min(4, nt - t0)) for t0 in range(0, nt, 4)]

    def over_chunks(eng, body):
        with eng.Fori(0, nch // 2) as v:
            for p in range(2):
                body(2 * v + p, v, p)
        if nch % 2:
            body(nch - 1, nch // 2, 0)

    with nc.Block() as block:

        @block.sync
        def _(sp):
            def store(c, v, p):
                for j in range(nt):
                    q = j % NS
                    sp.wait_ge(out_done[q], 2 * c + j // NS + 1)
                    sp.dma_start(out[(first + tiles[j]) * P:(first + tiles[j] + 1) * P, bass.ds((c + c0) * CH, CH)], stage[:, q, :]).then_inc(stored[q], 16)

            over_chunks(sp, store)
            for q in range(NS):
                sp.wait_ge(stored[q], 16 * 2 * nch)

        @block.scalar
        def _(act):
            if gates is not None:
                act.dma_start(wg[:], wg_src).then_inc(g_ld, 16)
                act.dma_start(gbias[:], gbias_src).then_inc(g_ld, 16)

            def load(c, v, p):
                act.wait_ge(lo_done, c)
                act.dma_start(wst[:], w_src[:, bass.ds((c + c0) * CH, CH)].rearrange("(k p) n -> p k n", p=P)).then_inc(w_ld, 16)
                act.wait_ge(w_ld, 16 * c + 16)
                act.wait_ge(used[p], v)
                nc.scalar.activation(whi[:, p], wst[:], ACT.Copy).then_inc(hi_done, 1)

            over_chunks(act, load)

        @block.gpsimd
        def _(pool):
            def split(c, v, p):
                pool.wait_ge(w_ld, 16 * c + 16)
                pool.wait_ge(hi_done, c + 1)
                nc.gpsimd.tensor_tensor(wlo[:, p], wst[:], whi[:, p].bitcast(F32), ALU.subtract).then_inc(lo_done, 1)

            over_chunks(pool, split)

        @block.vector
        def _(dve):
            if gates is not None:
                dve.wait_ge(g_ld, 32)
                nc.vector.tensor_copy(wg_hi[:], wg[:]).then_inc(g_split, 1)
                dve.wait_ge(g_split, 1)
                nc.vector.tensor_tensor(wg_lo[:], wg[:], wg_hi[:].bitcast(F32), ALU.subtract).then_inc(g_split, 1)
                for i, (t0, n) in enumerate(spans):
                    dve.wait_ge(g_mm, i + 1)
                    nc.vector.tensor_scalar(graw[:, (first + t0) * P:(first + t0 + n) * P], gacc[i % 2][:, 0:n * P], gbias[:], None, ALU.add).then_inc(g_out, 1)

            def out_of_psum(c, v, p):
                for j in range(nt):
                    q = j % NS
                    if j < nt - 1:
                        dve.wait_ge(mm_done[q], (2 if q < NS - 1 else 1) * c + j // NS + 1)
                    else:
                        dve.wait_ge(used[p], v + 1)
                    dve.wait_ge(stored[q], 16 * (2 * c + j // NS))
                    nc.vector.tensor_copy(stage[:, q, :], acc[q][:]).then_inc(out_done[q], 1)

            over_chunks(dve, out_of_psum)

        @block.tensor
        def _(pe):
            if gates is not None:
                pe.wait_ge(g_split, 2)
                for i, (t0, n) in enumerate(spans):
                    if i >= 2:
                        pe.wait_ge(g_out, i - 1)
                    for k in range(KD):
                        mm = split_mm(nc, gacc[i % 2][:, 0:n * P], wg_hi[:, k, :], wg_lo[:, k, :],
                                      h_hi[:, k, t0:t0 + n, :].rearrange("p t n -> p (t n)"), h_lo[:, k, t0:t0 + n, :].rearrange("p t n -> p (t n)"),
                                      k == 0, k == KD - 1)
                    mm.then_inc(g_mm, 1)

            def products(c, v, p):
                pe.wait_ge(lo_done, c + 1)
                for j in range(nt):
                    q = j % NS
                    pe.wait_ge(out_done[q], 2 * c + j // NS)
                    for k in range(KD):
                        mm = split_mm(nc, acc[q][:], h_hi[:, k, tiles[j], :], h_lo[:, k, tiles[j], :], whi[:, p, k, :], wlo[:, p, k, :], k == 0, k == KD - 1)
                    mm.then_inc(mm_done[q] if j < nt - 1 else used[p], 1)

            over_chunks(pe, products)


def projections(nc, m, a, s, keep, layer, graw):
    ncols = (W0_COLS, W1_COLS)[layer]
    x_src, w_src, out = ((a["x"], a["w0"], s["proj0"]), (s["x1"], a["w1"], s["proj1"]))[layer]
    for part, (first, count) in enumerate(PARTS):
        tag = f"pj{layer}{part}_"
        h_hi = m.sb(tag + "h_hi", [P, KD, count, P], F32R)
        h_lo = m.sb(tag + "h_lo", [P, KD, count, P], F32R)
        outer, m.stack = m.stack, ExitStack()
        normalised(nc, m, layer, x_src, keep["mod"], h_hi, h_lo, first, count, keep["ident"])
        m.end()
        wbuf = (m.sb(tag + "wst", [P, KD, CH]), m.sb(tag + "whi", [P, 2, KD, CH], F32R), m.sb(tag + "wlo", [P, 2, KD, CH], F32R))
        if layer == 0:
            projected(nc, m, tag, w_src, out, h_hi, h_lo, wbuf, range(ncols // CH), first, range(count))
        else:
            gates = (m.sb(tag + "wg", [P, KD, P]), m.sb(tag + "wg_hi", [P, KD, P], F32R), m.sb(tag + "wg_lo", [P, KD, P], F32R), graw,
                     m.sb(tag + "gbias", [P, 1]), a["w_gate"].rearrange("(k p) n -> p k n", p=P), a["gate_bias"])
            if part == 0:
                with_weights, m.stack = m.stack, ExitStack()
                projected(nc, m, tag, w_src, out, h_hi, h_lo, wbuf, range(0, 4), first, range(count), gates)
                m.free()
                m.stack = with_weights
                projected(nc, m, tag + "b", w_src, out, h_hi, h_lo, wbuf, range(4, 10), first, range(CT, count))
            else:
                projected(nc, m, tag, w_src, out, h_hi, h_lo, wbuf, range(0, 10), first, range(count), gates)
        m.end()
        m.stack = outer
        m.end()


def wait(eng, sem, base, n):
    if not (isinstance(n, int) and n <= 0):
        eng.wait_ge(sem, base + n)


def heads(nc, m, a, s, keep, kres, vres):
    NHD = NQ + NKV
    raw = m.sb("hd_raw", [P, 2, C_GATE])
    rope = m.sb("hd_rope", [P, 2, 2, 32])
    sq = m.sb("hd_sq", [P, C_GATE])
    ss = m.sb("hd_ss", [P, C_GATE // HD])
    rs = m.sb("hd_rs", [P, C_GATE // HD])
    nrm = m.sb("hd_nrm", [P, NHD, HD])
    un = m.sb("hd_un", [P, 2, FW])
    gq = m.sb("hd_gq", [P, D])
    gf = m.sb("hd_gf", [P, FW])
    half, eps = m.sb("hd_half", [P, C_GATE // HD]), m.sb("hd_eps", [P, C_GATE // HD])
    prod = m.sb("hd_prod", [P, 4, NHD, 32])
    rot = m.sb("hd_rot", [P, 2, NHD, HD])
    parts = m.sb("hd_parts", [P, NQ + 2 * NKV, P], F32R)
    qt = m.sb("hd_qt", [P, 2, NQ, P], F32R)
    NGR = (NQ + 2 * NKV) // 4
    tp = [m.ps(f"hd_tp{i}") for i in range(NGR)]
    const, ld = m.sem("hd_const"), m.sem("hd_ld", 2)
    raw_used = m.sem("hd_raw_used", 2)
    sq_done, ss_done, rs_done, ready = m.sem("hd_sq_done"), m.sem("hd_ss_done"), m.sem("hd_rs_done"), m.sem("hd_ready")
    chain, nrm_done, un_done, prod_done, rot_done = (m.sem("hd_" + x) for x in ("chain", "nrm_done", "un_done", "prod_done", "rot_done"))
    hi_done, lo_done = m.sem("hd_hi_done"), m.sem("hd_lo_done")
    tr_done, tr_out, stored, un_stored = m.sem("hd_tr", NGR), m.sem("hd_tr_out", NGR), m.sem("hd_stored", 2), m.sem("hd_un_stored", 2)
    ident = keep["ident"]
    bq = C_QK + D
    with nc.Block() as block:

        @block.sync
        def _(sp):
            sp.dma_start(gq[:], a["qk_gain"].broadcast_to([P, D])).then_inc(const, 16)
            sp.dma_start(gf[:], a["f_gain"].broadcast_to([P, FW])).then_inc(const, 16)
            with sp.Fori(0, NT // 2) as v:
                for p in range(2):
                    t = 2 * v + p
                    sp.wait_ge(raw_used[p], v)
                    sp.dma_start(raw[:, p, :], s["proj0"][bass.ds(t * P, P), 0:C_GATE]).then_inc(ld[p], 16)
                    sp.dma_start(rope[:, p], a["rope"][bass.ds(t * P, P)]).then_inc(ld[p], 16)

        @block.scalar
        def _(act):
            with act.Fori(0, NT // 2) as v:
                for p in range(2):
                    n = 2 * v + p
                    act.wait_ge(ld[p], 32 * v + 32)
                    act.wait_ge(ss_done, n)
                    nc.scalar.activation(sq[:], raw[:, p, :], ACT.Square).then_inc(sq_done, 1)
                    for g in range(NGR):
                        act.wait_ge(tr_done[g], n)
                    nc.scalar.activation(vres[:, n, :, 0:HD], raw[:, p, C_V:C_U].rearrange("p (h d) -> p h d", d=HD), ACT.Copy).then_inc(hi_done, 1)
                    act.wait_ge(rot_done, n + 1)
                    nc.scalar.activation(parts[:, 0:NHD, 0:HD], rot[:, p], ACT.Copy).then_inc(hi_done, 1)
                    nc.scalar.activation(parts[:, NQ:NHD, HD:P], rot[:, p, NQ:NHD, :], ACT.Copy).then_inc(hi_done, 1)
                    for g in (0, 2, 4):
                        act.wait_ge(tr_done[g], n + 1)
                        if g == 0:
                            act.wait_ge(stored[p], 16 * v)
                        src = tp[g][:].rearrange("p (h n) -> p h n", n=P)
                        dst = qt[:, p, 4 * g:4 * g + 4, :] if g < 3 else kres[:, 4 * (g - 3):4 * (g - 3) + 4, bass.ds(n * P, P)]
                        nc.scalar.activation(dst, src, ACT.Copy).then_inc(tr_out[g], 1)
                    act.wait_ge(tr_out[1], n + 1)
                    act.wait_ge(tr_out[2], n + 1)
                    act.dma_start(s["q"][:, n].rearrange("h p n -> p h n"), qt[:, p].bitcast(F32)).then_inc(stored[p], 16)
                    act.wait_ge(un_done, n + 1)
                    act.dma_start(s["un"][bass.ds(n * P, P), :], un[:, p, :]).then_inc(un_stored[p], 16)
            for p in range(2):
                act.wait_ge(stored[p], 16 * (NT // 2))
                act.wait_ge(un_stored[p], 16 * (NT // 2))

        @block.gpsimd
        def _(pool):
            nc.gpsimd.memset(half[:], -0.5).then_inc(ready, 1)
            nc.gpsimd.memset(eps[:], HD * EPS).then_inc(ready, 1)
            pool.wait_ge(ready, 2)
            with pool.Fori(0, NT // 2) as v:
                for p in range(2):
                    n = 2 * v + p
                    pool.wait_ge(ss_done, n + 1)
                    nc.gpsimd.tensor_tensor(rs[:], ss[:], eps[:], ALU.add).then_inc(ready, 1)
                    pool.wait_ge(ready, n + 3)
                    nc.gpsimd.tensor_tensor(rs[:], rs[:], half[:], ALU.pow).then_inc(rs_done, 1)
                    pool.wait_ge(nrm_done, n + 1)
                    pool.wait_ge(rot_done, n)
                    for i in range(2):
                        nc.gpsimd.tensor_tensor(prod[:, 2 + i], nrm[:, :, 32:64], rope[:, p, 1 - i, :].unsqueeze(1).broadcast_to([P, NHD, 32]), ALU.mult).then_inc(prod_done, 1)

        @block.vector
        def _(dve):
            dve.wait_ge(const, 32)
            nc.vector.tensor_scalar(gq[:], gq[:], float(HD) ** 0.5, None, ALU.mult).then_inc(const, 1)
            nc.vector.tensor_scalar(gf[:], gf[:], float(HD) ** 0.5, None, ALU.mult).then_inc(const, 1)
            dve.wait_ge(const, 34)
            with dve.Fori(0, NT // 2) as v:
                for p in range(2):
                    n = 2 * v + p
                    K = 5
                    c = Steps(dve, chain, n * K)
                    dve.wait_ge(sq_done, n + 1)
                    nc.vector.tensor_reduce(ss[:], sq[:].rearrange("p (h d) -> p h d", d=HD), AX.X, ALU.add).then_inc(ss_done, 1)
                    dve.wait_ge(rs_done, n + 1)
                    dve.wait_ge(prod_done, 2 * n)
                    c.did(nc.vector.tensor_tensor(nrm[:], raw[:, p, 0:bq].rearrange("p (h d) -> p h d", d=HD), rs[:, 0:NHD].unsqueeze(2).broadcast_to([P, NHD, HD]), ALU.mult))
                    c.wait()
                    nc.vector.tensor_tensor(nrm[:], nrm[:], gq[:].rearrange("p (h d) -> p h d", d=HD), ALU.mult).then_inc(nrm_done, 1)
                    dve.wait_ge(un_stored[p], 16 * v)
                    c.did(nc.vector.tensor_tensor(un[:, p].rearrange("p (h d) -> p h d", d=HD), raw[:, p, C_U:C_GATE].rearrange("p (h d) -> p h d", d=HD),
                                                  rs[:, C_U // HD:].unsqueeze(2).broadcast_to([P, FW // HD, HD]), ALU.mult))
                    dve.wait_ge(nrm_done, n + 1)
                    for i in range(2):
                        c.did(nc.vector.tensor_tensor(prod[:, i], nrm[:, :, 0:32], rope[:, p, i, :].unsqueeze(1).broadcast_to([P, NHD, 32]), ALU.mult))
                    c.wait()
                    nc.vector.tensor_tensor(un[:, p], un[:, p], gf[:], ALU.mult).then_inc(un_done, 1)
                    dve.wait_ge(prod_done, 2 * n + 2)
                    c.did(nc.vector.tensor_tensor(rot[:, p, :, 0:32], prod[:, 0], prod[:, 2], ALU.subtract))
                    nc.vector.tensor_tensor(rot[:, p, :, 32:64], prod[:, 1], prod[:, 3], ALU.add).then_inc(rot_done, 1)
                    assert c.n == K
                    dve.wait_ge(hi_done, 3 * n + 1)
                    nc.vector.tensor_tensor(vres[:, n, :, HD:P], raw[:, p, C_V:C_U].rearrange("p (h d) -> p h d", d=HD), vres[:, n, :, 0:HD].bitcast(F32), ALU.subtract).then_inc(raw_used[p], 1)
                    dve.wait_ge(hi_done, 3 * n + 3)
                    dve.wait_ge(rot_done, n + 1)
                    nc.vector.tensor_tensor(parts[:, 0:NQ, HD:P], rot[:, p, 0:NQ, :], parts[:, 0:NQ, 0:HD].bitcast(F32), ALU.subtract).then_inc(lo_done, 1)
                    for i in range(2):
                        nc.vector.tensor_tensor(parts[:, NHD:, i * HD:(i + 1) * HD], rot[:, p, NQ:NHD, :], parts[:, NQ:NHD, 0:HD].bitcast(F32), ALU.subtract).then_inc(lo_done, 1)
                    for g in (1, 3):
                        dve.wait_ge(tr_done[g], n + 1)
                        src = tp[g][:].rearrange("p (h n) -> p h n", n=P)
                        dst = qt[:, p, 4 * g:4 * g + 4, :] if g < 3 else kres[:, 4 * (g - 3):4 * (g - 3) + 4, bass.ds(n * P, P)]
                        nc.vector.tensor_copy(dst, src).then_inc(tr_out[g], 1)

        @block.tensor
        def _(pe):
            with pe.Fori(0, NT // 2) as v:
                for p in range(2):
                    n = 2 * v + p
                    pe.wait_ge(lo_done, 3 * n + 3)
                    for g in range(NGR):
                        pe.wait_ge(tr_out[g], n)
                        for i in range(4):
                            tr = nc.tensor.transpose(tp[g][:, i * P:(i + 1) * P], parts[:, 4 * g + i, :].bitcast(F32), ident[:])
                        tr.then_inc(tr_done[g], 1)


def attention(nc, m, a, s, keep, kres, vres, tag, q0, nq, nk):
    groups = [(4 * b, min(4, nk - 4 * b)) for b in range((nk + 3) // 4)]
    G, M = len(groups), QPK * nq
    V = M // 2
    q = m.sb(tag + "q", [P, 2, P], F32R)
    e = m.sb(tag + "e", [P, 2, nk * P])
    e_hi = m.sb(tag + "e_hi", [P, nk, 2, P], F32R)
    e_lo = m.sb(tag + "e_lo", [P, nk, 2, P], F32R)
    vcur = m.sb(tag + "vcur", [P, nk, P], F32R)
    mx = m.sb(tag + "mx", [P, G + 1])
    nbias = m.sb(tag + "nbias", [P, 2])
    esum = m.sb(tag + "esum", [P, 2, G])
    tot = m.sb(tag + "tot", [P, 2])
    rden = m.sb(tag + "rden", [P, 2])
    ot = m.sb(tag + "ot", [P, 2, P])
    o = m.sb(tag + "o", [P, 2, HD])
    fold = m.sb(tag + "fold", [P, P])
    sc = [m.ps(tag + f"sc{b}") for b in range(G)]
    tp = [m.ps(tag + f"tp{i}") for i in range(2)]
    acc = m.ps(tag + "acc")
    fold_ld, v_done = m.sem(tag + "fold_ld"), m.sem(tag + "v")
    q_ld, s_done, mx_done, bias_done = m.sem(tag + "q_ld", 2), m.sem(tag + "s"), m.sem(tag + "mx"), m.sem(tag + "bias")
    e_done, t_done, hi_done, lo_done = m.sem(tag + "e"), m.sem(tag + "t"), m.sem(tag + "hi"), m.sem(tag + "lo")
    pv_done, r_done, ot_done, fold_done = m.sem(tag + "pv"), m.sem(tag + "r"), m.sem(tag + "ot"), m.sem(tag + "fold")
    o_done, stored = m.sem(tag + "o"), m.sem(tag + "stored", 2)
    scale = HD ** -0.5
    own = {b + 2: b for b in range(G - 2)}
    later = {i: b for i, b in enumerate(range(max(G - 2, 0), G))}
    OUT_AT, FOLD_AT, NORM_AT = min(2, G - 1), min(3, G - 1), G - 1

    def over_heads(eng, before, body, after):
        with eng.Fori(0, NKV) as g:
            eng.wait_ge(o_done, g * M)
            before(g)
            for p in range(2):
                body(g, p, p, 0)
            if V > 2:
                with eng.Fori(1, V - 1) as v:
                    for p in range(2):
                        body(g, 2 * v + p, p, v)
            for p in range(2):
                body(g, M - 2 + p, p, V - 1)
            after(g)

    none = lambda g: None
    fixed = lambda i: isinstance(i, int)
    is_last = lambda i: fixed(i) and i == M - 1
    in_first = lambda i: fixed(i) and i < 2
    with nc.Block() as block:

        @block.sync
        def _(sp):
            sp.dma_start(fold[:], a["fold"]).then_inc(fold_ld, 16)

            def load(g, i, p):
                sp.dma_start(q[:, p, :].bitcast(F32), s["q"][QPK * g + i // nq, i % nq + q0]).then_inc(q_ld[p], 16)

            def store(g, i, p):
                sp.wait_ge(o_done, g * M + i + 1)
                sp.dma_start(s["attn"][bass.ds((i % nq + q0) * P, P), bass.ds((QPK * g + i // nq) * HD, HD)], o[:, p, :]).then_inc(stored[p], 16)

            def before(g):
                for p in range(2):
                    load(g, p, p)

            def body(g, i, p, v):
                if not (fixed(i) and i >= M - 2):
                    sp.wait_ge(s_done, (g * M + i + 1) * G)
                    load(g, i + 2, p)
                if p == 1 and not in_first(i):
                    for k in range(2):
                        store(g, i - 3 + k, k)

            def after(g):
                for k in range(2):
                    store(g, M - 2 + k, k)

            over_heads(sp, before, body, after)
            for p in range(2):
                sp.wait_ge(stored[p], 16 * V * NKV)

        @block.scalar
        def _(act):
            def hi(g, i, p, v, b):
                t0, w = groups[b]
                act.wait_ge(t_done, (g * M + i) * G + b + 1)
                wait(act, pv_done, (g * V + v - 1) * G, b + 1 if not in_first(i) else 0)
                nc.scalar.activation(e_hi[:, t0:t0 + w, p, :], tp[(p * G + b) % 2][:, 0:w * P].rearrange("p (t n) -> p t n", n=P), ACT.Copy).then_inc(hi_done, 1)

            def out(g, v):
                act.wait_ge(pv_done, (g * V + v + 1) * G)
                nc.scalar.activation(ot[:], acc[:, 0:2 * P].rearrange("p (t n) -> p t n", n=P), ACT.Copy).then_inc(ot_done, 1)

            def body(g, i, p, v):
                act.wait_ge(bias_done, g * M + i + 1)
                for b, (t0, w) in enumerate(groups):
                    wait(act, t_done, (g * M + i - 2) * G, b + 1 if not in_first(i) else 0)
                    if b == 0 and not in_first(i):
                        act.wait_ge(r_done, 2 * (g * M + i - 1))
                    nc.scalar.activation(e[:, p, t0 * P:(t0 + w) * P], sc[b][:, 0:w * P], ACT.Exp, bias=nbias[:, p:p + 1], scale=scale,
                                         accum_out=esum[:, p, b:b + 1]).then_inc(e_done, 1)
                    if b:
                        hi(g, i, p, v, b - 1)
                    if p == 0 and b == OUT_AT and not in_first(i):
                        out(g, v - 1)
                hi(g, i, p, v, G - 1)

            over_heads(act, none, body, lambda g: out(g, V - 1))

        @block.vector
        def _(dve):
            dve.wait_ge(fold_ld, 16)

            def maximum(g, i, b):
                dve.wait_ge(s_done, (g * M + i) * G + b + 1)
                nc.vector.reduce_max(mx[:, b:b + 1], sc[b][:, 0:groups[b][1] * P], AX.X).then_inc(mx_done, 1)

            def bias(g, i, p):
                n = (g * M + i) * (G + 1)
                dve.wait_ge(mx_done, n + G)
                nc.vector.reduce_max(mx[:, G:G + 1], mx[:, 0:G], AX.X).then_inc(mx_done, 1)
                dve.wait_ge(mx_done, n + G + 1)
                nc.vector.tensor_scalar(nbias[:, p:p + 1], mx[:, G:G + 1], -scale, None, ALU.mult).then_inc(bias_done, 1)

            def lo(g, i, p, b):
                t0, w = groups[b]
                dve.wait_ge(hi_done, (g * M + i) * G + b + 1)
                nc.vector.tensor_tensor(e_lo[:, t0:t0 + w, p, :], tp[(p * G + b) % 2][:, 0:w * P].rearrange("p (t n) -> p t n", n=P), e_hi[:, t0:t0 + w, p, :].bitcast(F32), ALU.subtract).then_inc(lo_done, 1)

            def denominator(g, i, p):
                n = 2 * (g * M + i)
                dve.wait_ge(e_done, (g * M + i + 1) * G)
                nc.vector.reduce_sum(tot[:, p:p + 1], esum[:, p, :], AX.X).then_inc(r_done, 1)
                dve.wait_ge(r_done, n + 1)
                nc.vector.reciprocal(rden[:, p:p + 1], tot[:, p:p + 1]).then_inc(r_done, 1)

            def norm(g, v):
                dve.wait_ge(fold_done, g * V + v + 1)
                dve.wait_ge(r_done, 2 * (g * M + 2 * v + 2))
                for p in range(2):
                    dve.wait_ge(stored[p], 16 * (g * V + v))
                    nc.vector.tensor_scalar(o[:, p, :], acc[:, (2 + p) * P:(2 + p) * P + HD], rden[:, p:p + 1], None, ALU.mult).then_inc(o_done, 1)

            def before(g):
                nc.vector.tensor_copy(vcur[:], vres[:, 0:nk, g, :].bitcast(F32)).then_inc(v_done, 1)
                for b in range(G):
                    maximum(g, 0, b)
                bias(g, 0, 0)

            def body(g, i, p, v):
                for b in range(G):
                    if not is_last(i):
                        maximum(g, i + 1, b)
                        if b == G - 1:
                            bias(g, i + 1, 1 - p)
                    lo(g, i, p, b)
                    if p == 0 and b == NORM_AT and not in_first(i):
                        norm(g, v - 1)
                denominator(g, i, p)

            over_heads(dve, before, body, lambda g: norm(g, V - 1))

        @block.tensor
        def _(pe):
            pe.wait_ge(fold_ld, 16)

            def scores(g, i, p, v, b):
                t0, w = groups[b]
                if b == 0:
                    pe.wait_ge(q_ld[p], 16 * (g * V + v + 1))
                wait(pe, e_done, (g * M + i - 1) * G, b + 1 if not (fixed(i) and i == 0) else 0)
                for k in range(2):
                    mm = nc.tensor.matmul(sc[b][:, 0:w * P], q[:, p, :], kres[:, g + NKV * k, t0 * P:(t0 + w) * P], start=(k == 0), stop=(k == 1))
                mm.then_inc(s_done, 1)

            def turned(g, i, p, b):
                t0, w = groups[b]
                pe.wait_ge(e_done, (g * M + i) * G + b + 1)
                wait(pe, lo_done, (g * M + i) * G - 1, b if not (fixed(i) and i * G + b < 2) else 0)
                for t in range(w):
                    mm = nc.tensor.transpose(tp[(p * G + b) % 2][:, t * P:(t + 1) * P], e[:, p, (t0 + t) * P:(t0 + t + 1) * P], keep["ident"][:])
                mm.then_inc(t_done, 1)

            def values(g, v, b):
                t0, w = groups[b]
                pe.wait_ge(lo_done, (g * M + 2 * v + 1) * G + b + 1)
                if b == 0:
                    pe.wait_ge(v_done, g + 1)
                    pe.wait_ge(o_done, g * M + 2 * v)
                for t in range(t0, t0 + w):
                    nc.tensor.matmul(acc[:, 0:2 * P], vcur[:, t, :], e_hi[:, t].rearrange("p a n -> p (a n)"), start=(t == 0), stop=False)
                    mm = nc.tensor.matmul(acc[:, 0:2 * P], vcur[:, t, :], e_lo[:, t].rearrange("p a n -> p (a n)"), start=False, stop=(t == nk - 1))
                mm.then_inc(pv_done, 1)

            def folded(g, v):
                pe.wait_ge(ot_done, g * V + v + 1)
                for p in range(2):
                    mm = nc.tensor.matmul(acc[:, (2 + p) * P:(3 + p) * P], ot[:, p, :], fold[:], start=True, stop=True)
                mm.then_inc(fold_done, 1)

            def before(g):
                for b in range(G):
                    scores(g, 0, 0, 0, b)

            def body(g, i, p, v):
                for b in range(G):
                    if not is_last(i):
                        scores(g, i + 1, 1 - p, v + p, b)
                    if p == 1 and b in own:
                        values(g, v, own[b])
                    if p == 0 and b in later and not in_first(i):
                        values(g, v - 1, later[b])
                    turned(g, i, p, b)
                    if p == 0 and b == FOLD_AT and not in_first(i):
                        folded(g, v - 1)

            def after(g):
                for b in later.values():
                    values(g, V - 1, b)
                folded(g, V - 1)

            over_heads(pe, before, body, after)


def fourier(nc, m, a, s, keep):
    jobs = ((0, CT, "dft_ctx"), (CT, LT, "dft_lat"))
    H = LT // 2
    u = m.sb("fo_u", [P, NT, FW])
    ev, od = m.sb("fo_ev", [P, H - 1, FW]), m.sb("fo_od", [P, H - 1, FW])
    z = m.sb("fo_z", [P, H + 1 + 2, 3, FW])
    tabs = [m.sb("fo_" + name, [P, 2, R, P]) for _, R, name in jobs]
    head_tab, mix = m.sb("fo_head", [P, 2, P]), m.sb("fo_mix", [P, 2, P])
    g12 = m.sb("fo_g", [P, 2, 2, P])
    yt = m.sb("fo_yt", [P, 2, 4, P])
    o = m.sb("fo_o", [P, 2, FW])
    pg, py, po = m.ps("fo_pg"), [m.ps(f"fo_py{i}") for i in range(2)], [m.ps(f"fo_po{i}") for i in range(2)]
    ld, chain, z_done = m.sem("fo_ld"), m.sem("fo_chain"), m.sem("fo_z_done")
    g_mm, g_done = m.sem("fo_g_mm"), m.sem("fo_g_done")
    y_mm, y_out, o_mm, o_out, stored = m.sem("fo_y_mm"), m.sem("fo_y_out"), m.sem("fo_o_mm"), m.sem("fo_o_out"), m.sem("fo_stored", 2)
    outs = [(j, R, r, (H + 1 + r if j == 0 else min(r, R - r)), j == 1 and r > H) for j, (_, R, _) in enumerate(jobs) for r in range(R)]
    with nc.Block() as block:

        @block.sync
        def _(sp):
            sp.dma_start(head_tab[:], a["dft_head"].rearrange("c p n -> p c n")).then_inc(ld, 16)
            sp.dma_start(mix[:], a["fmix"].rearrange("c p n -> p c n")).then_inc(ld, 16)
            sp.dma_start(u[:], s["un"].rearrange("(t p) n -> p t n", p=P)).then_inc(ld, 16)
            for tab, (_, _, name) in zip(tabs, jobs):
                sp.dma_start(tab[:], a[name]).then_inc(ld, 16)
            for n, (j, R, r, _, _) in enumerate(outs):
                sp.wait_ge(o_out, n + 1)
                rows = s["four"][0:CTX] if j == 0 else s["four"][CTX:T]
                sp.dma_start(rows.rearrange("(m r) c -> r m c", r=R)[r], o[:, n % 2, :]).then_inc(stored[n % 2], 16)
            for i in range(2):
                sp.wait_ge(stored[i], 16 * (len(outs) // 2))

        @block.vector
        def _(dve):
            dve.wait_ge(ld, 80)
            c = Steps(dve, chain)
            c.did(nc.vector.tensor_tensor(z[:, H + 1, 0, :], u[:, 0], u[:, 1], ALU.add))
            c.did(nc.vector.tensor_tensor(z[:, H + 2, 0, :], u[:, 0], u[:, 1], ALU.subtract))
            x = u[:, CT:]
            c.did(nc.vector.tensor_tensor(ev[:], x[:, 1:H], x[:, LT - 1:H:-1], ALU.add))
            c.did(nc.vector.tensor_tensor(od[:], x[:, 1:H], x[:, LT - 1:H:-1], ALU.subtract))
            for r in range(H + 1):
                c.did(nc.vector.tensor_tensor(z[:, r, 0, :], x[:, 0], x[:, H], ALU.add if r % 2 == 0 else ALU.subtract))
            c.did(nc.vector.memset(z[:, 0:H + 1:H, 1:3, :], 0.0))
            for i in range(1, H):
                c.wait()
                for r in range(H + 1):
                    co = float(np.cos(2 * np.pi * ((i * r) % LT) / LT))
                    c.did(nc.vector.scalar_tensor_tensor(z[:, r, 0, :], ev[:, i - 1], co, z[:, r, 0, :], ALU.mult, ALU.add))
                for r in range(1, H):
                    si = -float(np.sin(2 * np.pi * ((i * r) % LT) / LT))
                    if i == 1:
                        c.did(nc.vector.tensor_scalar(z[:, r, 1, :], od[:, 0], si, None, ALU.mult))
                    else:
                        c.did(nc.vector.scalar_tensor_tensor(z[:, r, 1, :], od[:, i - 1], si, z[:, r, 1, :], ALU.mult, ALU.add))
            c.wait()
            nc.vector.tensor_scalar(z[:, 1:H, 2, :], z[:, 1:H, 1, :], -1.0, None, ALU.mult).then_inc(z_done, 1)
            for n in range(len(outs)):
                dve.wait_ge(o_mm, n + 1)
                if n >= 2:
                    dve.wait_ge(stored[n % 2], 16 * (n // 2))
                nc.vector.tensor_copy(o[:, n % 2, :], po[n % 2][:, 0:FW]).then_inc(o_out, 1)

        @block.scalar
        def _(act):
            act.wait_ge(g_mm, 1)
            nc.scalar.activation(g12[:], pg[:].rearrange("p (c h n) -> p c h n", c=2, h=2), ACT.Copy).then_inc(g_done, 1)
            for n in range(len(outs)):
                act.wait_ge(y_mm, n + 1)
                if n >= 2:
                    act.wait_ge(o_mm, n - 1)
                nc.scalar.activation(yt[:, n % 2], py[n % 2][:].rearrange("p (c n) -> p c n", c=4), ACT.Copy).then_inc(y_out, 1)

        @block.tensor
        def _(pe):
            pe.wait_ge(ld, 80)
            for c in range(2):
                for h in range(2):
                    mm = nc.tensor.matmul(pg[:, (2 * c + h) * P:(2 * c + h + 1) * P], head_tab[:, c, :], mix[:, h, :], start=True, stop=True)
            mm.then_inc(g_mm, 1)
            pe.wait_ge(z_done, 1)

            def mixed(n):
                pe.wait_ge(y_out, n + 1)
                if n == 0:
                    pe.wait_ge(g_done, 1)
                if n >= 2:
                    pe.wait_ge(o_out, n - 1)
                for h in range(2):
                    for c in range(2):
                        mm = nc.tensor.matmul(po[n % 2][:, h * P:(h + 1) * P], yt[:, n % 2, 2 * h + c, :], g12[:, c, h, :], start=(c == 0), stop=(c == 1))
                mm.then_inc(o_mm, 1)

            for n, (j, R, r, slot, conj) in enumerate(outs):
                if n >= 2:
                    pe.wait_ge(y_out, n - 1)
                co, si = tabs[j][:, 0, r, :], tabs[j][:, 1, r, :]
                re, im, nim = (z[:, slot, i, :] for i in range(3))
                if conj:
                    im, nim = nim, im
                for h in range(2):
                    cols = slice(h * P, (h + 1) * P)
                    for c, terms in enumerate((((re, co), (im, si)), ((re, si), (nim, co)))):
                        if j == 0:
                            terms = terms[:1]
                        dst = py[n % 2][:, (2 * h + c) * P:(2 * h + c + 1) * P]
                        for i, (lhs, rhs) in enumerate(terms):
                            mm = nc.tensor.matmul(dst, lhs[:, cols], rhs, start=(i == 0), stop=(i == len(terms) - 1))
                mm.then_inc(y_mm, 1)
                if n:
                    mixed(n - 1)
            mixed(len(outs) - 1)


def mixer_out(nc, m, a, s, keep, layer, out):
    L0 = layer == 0
    tag = f"mo{layer}_"
    t0 = 0 if L0 else CT
    N = NT - t0
    w = a["w_out0"] if L0 else a["w_out1"]
    x_src = a["x"] if L0 else s["x1"]
    NIN = 2 if L0 else 4
    ins = m.sb(tag + "in", [P, 2, NIN, D])
    x = m.sb(tag + "x", [P, 2, D])
    sg = m.sb(tag + "sg", [P, NIN // 2, D])
    y = m.sb(tag + "y", [P, 2, D])
    y_hi, y_lo = m.sb(tag + "y_hi", [P, 2, KD, P], F32R), m.sb(tag + "y_lo", [P, 2, KD, P], F32R)
    wst = m.sb(tag + "wst", [P, KD, CH])
    whi, wlo = m.sb(tag + "whi", [P, KD, D], F32R), m.sb(tag + "wlo", [P, KD, D], F32R)
    gate = m.sb(tag + "gate", [P, 2 if L0 else 1, D])
    gain, beta = m.sb(tag + "gain", [P, D]), m.sb(tag + "beta", [P, D])
    r = m.sb(tag + "r", [P, D])
    fin = m.sb(tag + "fin", [P, 2, D])
    eps, held = m.sb(tag + "eps", [P, 1]), m.sb(tag + "held", [P, 1])
    stats, mv, rstd, half = m.sb(tag + "stats", [P, 2, 6]), m.sb(tag + "mv", [P, 2]), m.sb(tag + "rstd", [P, 1]), m.sb(tag + "half", [P, 1])
    tp, acc = [m.ps(tag + f"tp{i}", (P, 2, 512)) for i in range(2)], [m.ps(tag + f"acc{i}", (P, 2, 512)) for i in range(2)]
    const, w_ld, w_hi, w_lo = m.sem(tag + "const"), m.sem(tag + "w_ld"), m.sem(tag + "w_hi"), m.sem(tag + "w_lo")
    in_ld, x_ld, y_done, x_used = m.sem(tag + "in_ld", 2), m.sem(tag + "x_ld", 2), m.sem(tag + "y_done", 2), m.sem(tag + "x_used", 2)
    sg_done, tr_done, hi_done, lo_done = m.sem(tag + "sg_done"), m.sem(tag + "tr"), m.sem(tag + "hi"), m.sem(tag + "lo")
    mm_done, chain, var_done, rstd_done = m.sem(tag + "mm"), m.sem(tag + "chain"), m.sem(tag + "var"), m.sem(tag + "rstd_d")
    nrm_done, fin_done, stored, ready, h_sum, zz = m.sem(tag + "nrm"), m.sem(tag + "fin"), m.sem(tag + "stored", 2), m.sem(tag + "ready"), m.sem(tag + "hsum"), m.sem(tag + "zz")
    acc_out = m.sem(tag + "acc_out")

    def over_tiles(eng, body, after=None):
        for p in range(2):
            body(p, p, 0)
        with eng.Fori(1, N // 2) as v:
            for p in range(2):
                body(2 * v + p, p, v)
        if after:
            after(N - 1, 1, N // 2 - 1)

    first = lambda n: isinstance(n, int) and n == 0
    with nc.Block() as block:

        @block.sync
        def _(sp):
            sp.dma_start(gain[:], a["post_gain"][layer:layer + 1].broadcast_to([P, D])).then_inc(const, 16)
            sp.dma_start(beta[:], a["post_bias"][layer:layer + 1].broadcast_to([P, D])).then_inc(const, 16)
            for i in range(2 if L0 else 1):
                sp.dma_start(gate[:, i, :], s["gates"][2 * layer + i]).then_inc(const, 16)

            def body(n, p, v):
                sp.wait_ge(y_done[p], v)
                rows = bass.ds((n + t0) * P, P)
                if L0:
                    sp.dma_start(ins[:, p, 0, 0:QW], s["attn"][rows, :]).then_inc(in_ld[p], 16)
                    sp.dma_start(ins[:, p, 0, QW:D], s["four"][rows, :]).then_inc(in_ld[p], 16)
                    sp.dma_start(ins[:, p, 1, :], s["proj0"][rows, C_GATE:W0_COLS]).then_inc(in_ld[p], 16)
                else:
                    for d in range(2):
                        sp.dma_start(ins[:, p, d, :], s["h"][d, bass.ds(n * P, P), :]).then_inc(in_ld[p], 16)
                    sp.dma_start(ins[:, p, 2:4, :], s["proj1"][rows, C1_O:W1_COLS].rearrange("p (i n) -> p i n", i=2)).then_inc(in_ld[p], 16)
                sp.wait_ge(x_used[p], v)
                sp.dma_start(x[:, p, :], x_src[rows, :]).then_inc(x_ld[p], 16)
                if first(n):
                    for h in range(2):
                        if h:
                            sp.wait_ge(w_lo, 1)
                        sp.dma_start(wst[:], w[:, h * CH:(h + 1) * CH].rearrange("(k p) n -> p k n", p=P)).then_inc(w_ld, 16)

            over_tiles(sp, body)

        @block.scalar
        def _(act):
            act.wait_ge(const, 16 * (4 if L0 else 3))
            fn = ACT.Silu if L0 else ACT.Sigmoid

            def body(n, p, v):
                act.wait_ge(in_ld[p], 48 * v + 48)
                if not first(n):
                    act.wait_ge(y_done[1 - p], v + p)
                nc.scalar.activation(sg[:], ins[:, p, NIN // 2:NIN, :], fn).then_inc(sg_done, 1)
                act.wait_ge(tr_done, n + 1)
                if not (isinstance(n, int) and n < 2):
                    act.wait_ge(mm_done, n - 1)
                nc.scalar.activation(y_hi[:, p], tp[p][:].rearrange("p a (k n) -> p (a k) n", n=P), ACT.Copy).then_inc(hi_done, 1)

            over_tiles(act, body)

        @block.gpsimd
        def _(pool):
            nc.gpsimd.memset(half[:], -0.5).then_inc(ready, 1)
            nc.gpsimd.memset(eps[:], EPS).then_inc(ready, 1)
            pool.wait_ge(ready, 2)
            pool.wait_ge(const, 16 * (4 if L0 else 3))

            def post(n, p, v):
                pool.wait_ge(var_done, n + 1)
                nc.gpsimd.tensor_tensor(rstd[:], mv[:, 1:2], eps[:], ALU.add).then_inc(ready, 1)
                pool.wait_ge(ready, n + 3)
                nc.gpsimd.tensor_tensor(rstd[:], rstd[:], half[:], ALU.pow).then_inc(rstd_done, 1)
                pool.wait_ge(nrm_done, n + 1)
                nc.gpsimd.tensor_tensor(fin[:, p, :], fin[:, p, :], beta[:], ALU.add).then_inc(fin_done, 1)
                pool.wait_ge(fin_done, n + 1)
                rows = out[bass.ds(n * P, P), :]
                pool.dma_start(rows, fin[:, p, :]).then_inc(stored[p], 16)

            def body(n, p, v):
                if not L0:
                    pool.wait_ge(sg_done, n + 1)
                    nc.gpsimd.tensor_tensor(ins[:, p, 3, :], ins[:, p, 3, :], sg[:, 1, :], ALU.mult).then_inc(zz, 1)
                if not first(n):
                    post(n - 1, 1 - p, v - 1 + p)

            over_tiles(pool, body, post)
            for p in range(2):
                pool.wait_ge(stored[p], 16 * (N // 2))

        @block.vector
        def _(dve):
            for h in range(2):
                dve.wait_ge(w_ld, 16 * (h + 1))
                nc.vector.tensor_copy(whi[:, :, h * CH:(h + 1) * CH], wst[:]).then_inc(w_hi, 1)
                dve.wait_ge(w_hi, h + 1)
                nc.vector.tensor_tensor(wlo[:, :, h * CH:(h + 1) * CH], wst[:], whi[:, :, h * CH:(h + 1) * CH].bitcast(F32), ALU.subtract).then_inc(w_lo, 1)
            dve.wait_ge(const, 16 * (4 if L0 else 3))
            K = 3

            def post(n, p, v):
                kind = (n * -1 + (NT + CT - 1)) // NT if L0 else 0
                c = Steps(dve, chain, n * K)
                dve.wait_ge(mm_done, n + 1)
                dve.wait_ge(nrm_done, n)
                nc.vector.tensor_tensor(r[:], acc[p][:].rearrange("p a n -> p (a n)"), gate[:, kind, :], ALU.mult).then_inc(acc_out, 1)
                dve.wait_ge(acc_out, n + 1)
                dve.wait_ge(x_ld[p], 16 * v + 16)
                nc.vector.scalar_tensor_tensor(r[:], x[:, p, :], ALPHA, r[:], ALU.mult, ALU.add).then_inc(x_used[p], 1)
                dve.wait_ge(x_used[p], v + 1)
                for h in range(2):
                    c.did(nc.vector.bn_stats(stats[:, h, :], r[:, h * 512:(h + 1) * 512]))
                c.wait()
                nc.vector.memset(held[:], 0.0)
                nc.vector.bn_aggr(mv[:], stats[:].rearrange("p a b -> p (a b)")).then_inc(var_done, 1)
                dve.wait_ge(rstd_done, n + 1)
                c.did(nc.vector.tensor_scalar(r[:], r[:], mv[:, 0:1], rstd[:], ALU.subtract, ALU.mult))
                c.wait()
                dve.wait_ge(stored[p], 16 * v)
                nc.vector.tensor_tensor(fin[:, p, :], r[:], gain[:], ALU.mult).then_inc(nrm_done, 1)
                assert c.n == K

            def body(n, p, v):
                dve.wait_ge(in_ld[p], 48 * v + 48)
                dve.wait_ge(sg_done, n + 1)
                if not (isinstance(n, int) and n < 2):
                    dve.wait_ge(tr_done, n - 1)
                if L0:
                    nc.vector.tensor_tensor(y[:, p, :], ins[:, p, 0, :], sg[:, 0, :], ALU.mult).then_inc(y_done[p], 1)
                else:
                    nc.vector.tensor_tensor(ins[:, p, 0, :], ins[:, p, 0, :], ins[:, p, 1, :], ALU.add).then_inc(h_sum, 1)
                    dve.wait_ge(h_sum, 2 * n + 1)
                    nc.vector.tensor_tensor(ins[:, p, 0, :], ins[:, p, 0, :], sg[:, 0, :], ALU.mult).then_inc(h_sum, 1)
                    dve.wait_ge(h_sum, 2 * n + 2)
                    dve.wait_ge(zz, n + 1)
                    nc.vector.tensor_tensor(y[:, p, :], ins[:, p, 0, :], ins[:, p, 3, :], ALU.mult).then_inc(y_done[p], 1)
                dve.wait_ge(hi_done, n + 1)
                nc.vector.tensor_tensor(y_lo[:, p], tp[p][:].rearrange("p a (k n) -> p (a k) n", n=P), y_hi[:, p].bitcast(F32), ALU.subtract).then_inc(lo_done, 1)
                if not first(n):
                    post(n - 1, 1 - p, v - 1 + p)

            over_tiles(dve, body, post)

        @block.tensor
        def _(pe):
            def products(n, p):
                if first(n):
                    pe.wait_ge(w_lo, 2)
                pe.wait_ge(lo_done, n + 1)
                if not (isinstance(n, int) and n < 2):
                    pe.wait_ge(acc_out, n - 1)
                for h in range(2):
                    for k in range(KD):
                        mm = split_mm(nc, acc[p][:, h, :], y_hi[:, p, k, :], y_lo[:, p, k, :], whi[:, k, h * CH:(h + 1) * CH], wlo[:, k, h * CH:(h + 1) * CH], k == 0, k == KD - 1)
                mm.then_inc(mm_done, 1)

            def body(n, p, v):
                pe.wait_ge(y_done[p], v + 1)
                if not (isinstance(n, int) and n < 2):
                    pe.wait_ge(lo_done, n - 1)
                for k in range(KD):
                    tr = nc.tensor.transpose(tp[p][:, k // 4, (k % 4) * P:(k % 4 + 1) * P], y[:, p, k * P:(k + 1) * P], keep["ident"][:])
                tr.then_inc(tr_done, 1)
                if not first(n):
                    products(n - 1, 1 - p)

            over_tiles(pe, body, lambda n, p, v: products(n, p))
    m.end()


def gate_rows(nc, m, a, keep, graw, mrow, cols, dec):
    R = NR
    full = lambda n: m.sb("gr_" + n, [R, T])
    lf, rst, neg, cum, cmax, tmp = (full(n) for n in ("lf", "rst", "neg", "cum", "cmax", "tmp"))
    arrs = [m.sb("gr_arr0", [P, T]), m.sb("gr_arr1", [P, T])]
    small = lambda n: m.sb("gr_" + n, [R, NT])
    tot, amax, tot_t, amax_t, m_t, m_in_t, m_in, m_last = (small(n) for n in ("tot", "amax", "tot_t", "amax_t", "m_t", "m_in_t", "m_in", "m_last"))
    decr = m.sb("gr_decr", [P, NT])
    sel = m.sb("gr_sel", [P, 2 * MH, P])
    tp = [m.ps(f"gr_tp{i}") for i in range(2)]
    pd = m.ps("gr_pd")
    ld, ready, v_done, s_done = m.sem("gr_ld"), m.sem("gr_ready"), m.sem("gr_v"), m.sem("gr_s")
    diff_done, scaled = m.sem("gr_diff"), m.sem("gr_scaled")
    tr_done, tr_out, d_mm = m.sem("gr_tr"), m.sem("gr_tr_out"), m.sem("gr_d_mm")
    FW_, BW_ = slice(0, 32), slice(32, R)
    blocks = [(i, t0, min(4, NT - t0)) for i in range(2) for t0 in range(0, NT, 4)]
    ch = lambda ap: ap.rearrange("p (c n) -> p c n", n=P)
    bc = lambda ap: ap.unsqueeze(2).broadcast_to([R, NT, P])
    with nc.Block() as block:

        @block.sync
        def _(sp):
            sp.dma_start(sel[:], a["sel"]).then_inc(ld, 16)

        @block.gpsimd
        def _(pool):
            for t in (arrs[0], arrs[1], mrow, decr):
                nc.gpsimd.memset(t[:], 0.0).then_inc(ready, 1)

        @block.scalar
        def _(act):
            nc.scalar.activation(tmp[:], graw[64:64 + R, :], ACT.Abs).then_inc(s_done, 1)
            act.wait_ge(s_done, 1)
            nc.scalar.activation(tmp[:], tmp[:], ACT.Exp, scale=-1.0).then_inc(s_done, 1)
            act.wait_ge(s_done, 2)
            nc.scalar.activation(tmp[:], tmp[:], ACT.Ln, bias=1.0).then_inc(s_done, 1)
            for n, (dst, sc) in enumerate(((arrs[0][64:64 + R, :], 1.0), (arrs[1][0:R, :], 1.0), (arrs[1][64:64 + R, :], -1.0), (decr[0:R, :], 1.0))):
                act.wait_ge(diff_done, n + 1)
                nc.scalar.activation(dst, dst, ACT.Exp, scale=sc).then_inc(s_done, 1)

        @block.vector
        def _(dve):
            c = Steps(dve, v_done)

            def do(ins):
                c.did(ins)
                c.wait()

            V = nc.vector
            do(V.memset(rst[:], 1.0))
            do(V.memset(rst[FW_, 0::P], 0.0))
            do(V.memset(rst[BW_, P - 1::P], 0.0))
            do(V.tensor_scalar(neg[:], rst[:], -1.0, MASKED, ALU.add, ALU.mult))
            do(V.tensor_scalar(lf[:], graw[64:64 + R, :], 0.0, None, ALU.min))
            dve.wait_ge(s_done, 3)
            do(V.tensor_tensor(lf[:], lf[:], tmp[:], ALU.subtract))
            do(V.tensor_tensor_scan(cum[FW_, :], rst[FW_, :], lf[FW_, :], 0.0, ALU.mult, ALU.add))
            do(V.tensor_tensor_scan(cum[BW_, ::-1], rst[BW_, ::-1], lf[BW_, ::-1], 0.0, ALU.mult, ALU.add))
            dve.wait_ge(ready, 4)
            av = arrs[0][0:R, :]
            do(V.tensor_tensor(av, graw[0:R, :], cum[:], ALU.subtract))
            do(V.tensor_tensor_scan(cmax[FW_, :], neg[FW_, :], arrs[0][FW_, :], -MASKED, ALU.add, ALU.max))
            do(V.tensor_tensor_scan(cmax[BW_, ::-1], neg[BW_, ::-1], arrs[0][BW_, ::-1], -MASKED, ALU.add, ALU.max))
            for dst, src in ((tot, cum), (amax, cmax)):
                do(V.tensor_copy(dst[FW_, :], src[FW_, P - 1::P]))
                do(V.tensor_copy(dst[BW_, :], src[BW_, 0::P]))
            for dst, src in ((tot_t, tot), (amax_t, amax)):
                do(V.tensor_copy(dst[FW_, :], src[FW_, :]))
                do(V.tensor_copy(dst[BW_, 0:CT], src[BW_, CT - 1::-1]))
                do(V.tensor_copy(dst[BW_, CT:NT], src[BW_, NT - 1:CT - 1:-1]))
            do(V.tensor_tensor_scan(m_t[:], amax_t[:], tot_t[:], 0.0, ALU.max, ALU.add))
            do(V.memset(m_in_t[:, 0:1], 0.0))
            do(V.tensor_copy(m_in_t[:, 1:NT], m_t[:, 0:NT - 1]))
            do(V.tensor_copy(m_in[FW_, :], m_in_t[FW_, :]))
            do(V.tensor_copy(m_in[BW_, CT - 1::-1], m_in_t[BW_, 0:CT]))
            do(V.tensor_copy(m_in[BW_, NT - 1:CT - 1:-1], m_in_t[BW_, CT:NT]))
            do(V.tensor_tensor(m_last[:], m_in[:], amax[:], ALU.max))
            do(V.tensor_tensor(ch(mrow[0:R, :]), ch(cmax[:]), bc(m_in[:]), ALU.max))
            do(V.tensor_tensor(ch(cmax[:]), ch(av), bc(m_last[:]), ALU.subtract))
            V.tensor_copy(arrs[0][64:64 + R, :], cmax[:]).then_inc(diff_done, 1)
            V.tensor_tensor(ch(arrs[1][0:R, :]), bc(m_in[:]), ch(mrow[0:R, :]), ALU.subtract).then_inc(diff_done, 1)
            do(V.tensor_tensor(tmp[:], cum[:], mrow[0:R, :], ALU.add))
            V.tensor_copy(arrs[1][64:64 + R, :], tmp[:]).then_inc(diff_done, 1)
            V.tensor_tensor(decr[0:R, :], m_in[:], m_last[:], ALU.subtract).then_inc(diff_done, 1)
            dve.wait_ge(s_done, 4)
            V.tensor_scalar(arrs[0][64:64 + R, :], arrs[0][64:64 + R, :], float(MD) ** -0.5, None, ALU.mult).then_inc(scaled, 1)
            for n, (i, t0, w) in enumerate(blocks):
                dve.wait_ge(tr_done, n + 1)
                src = tp[n % 2][:, 0:w * P].rearrange("p (t g r) -> p t g r", g=4, r=32)
                for t in range(w):
                    V.tensor_copy(cols[:, t0 + t, i], src[:, t, :, 0:MH]).then_inc(tr_out, 1)
            dve.wait_ge(d_mm, 1)
            V.tensor_copy(dec[:], pd[:, 0:2 * MH * NT].rearrange("p (r c) -> p r c", c=NT)).then_inc(v_done, 1)

        @block.tensor
        def _(pe):
            out_n = 0
            for n, (i, t0, w) in enumerate(blocks):
                if n == 0:
                    pe.wait_ge(scaled, 1)
                if i == 1 and t0 == 0:
                    pe.wait_ge(s_done, 6)
                if n >= 2:
                    pe.wait_ge(tr_out, sum(b[2] for b in blocks[:n - 1]))
                for t in range(w):
                    tr = nc.tensor.transpose(tp[n % 2][:, t * P:(t + 1) * P], arrs[i][:, (t0 + t) * P:(t0 + t + 1) * P], keep["ident"][:])
                tr.then_inc(tr_done, 1)
            pe.wait_ge(s_done, 7)
            pe.wait_ge(ld, 16)
            for r in range(2 * MH):
                mm = nc.tensor.matmul(pd[:, r * NT:(r + 1) * NT], sel[:, r, :], decr[:], start=True, stop=True)
            mm.then_inc(d_mm, 1)


def mlstm(nc, m, a, s, keep, mrow, cols, dec):
    VC = MD + 2
    kb = m.sb("ml_k", [P, 2, 2, D])
    vb = m.sb("ml_v", [P, 2, 2, MH, VC])
    qb = m.sb("ml_q", [P, 2, 2, D])
    qkt = m.sb("ml_qkt", [P, 2, 4, P])
    ccol = m.sb("ml_ccol", [P, 2, 2, 2, 4, MH])
    dcol = m.sb("ml_dcol", [P, 2, 2, 2 * MH])
    dw, sw = m.sb("ml_dw", [P, 2, P]), m.sb("ml_sw", [P, 2, P])
    vw = m.sb("ml_vw", [P, 2, VC])
    state = m.sb("ml_state", [P, 2, MH, 2, VC])
    inter, total = m.sb("ml_inter", [P, 2, VC]), m.sb("ml_total", [P, 2, VC])
    den = m.sb("ml_den", [P, 3])
    h = m.sb("ml_h", [P, 2, 2, D])
    sel, mask = m.sb("ml_sel", [P, 2 * MH, P]), m.sb("ml_mask", [P, 2, P])
    tp = [m.ps(f"ml_tp{i}") for i in range(2)]
    psc, pmx, pin, pst = m.ps("ml_psc"), m.ps("ml_pmx"), m.ps("ml_pin"), m.ps("ml_pst")
    pup = m.ps("ml_pup", (P, 2, 512))
    const, ready = m.sem("ml_const"), m.sem("ml_ready")
    ld = [[m.sem(f"ml_ld{d}{p}") for p in range(2)] for d in range(2)]
    col_done, tr_done, tr_out, sc_mm, mx_mm = (m.sem("ml_" + x) for x in ("col", "tr", "tr_out", "sc", "mx"))
    dw_done, sw_done, in_mm, st_mm, up_mm, vw_done = (m.sem("ml_" + x) for x in ("dw", "sw", "in", "st", "up", "vw"))
    inter_done, total_done, den_done, h_done, up_half, up_done = (m.sem("ml_" + x) for x in ("inter", "total", "den", "h", "up_half", "up_done"))
    stored = [[m.sem(f"ml_stored{d}{p}") for p in range(2)] for d in range(2)]
    U = [(p, d, hh) for p in range(2) for d in range(2) for hh in range(MH)]
    NU = len(U)
    TURNS = LT // 2
    chunk = lambda v, p, d: CT + 2 * v + p if d == 0 else v * -2 + (NT - 1 - p)
    ctx_chunk = lambda p, d: p if d == 0 else CT - 1 - p
    with nc.Block() as block:

        @block.sync
        def _(sp):
            sp.dma_start(sel[:], a["sel"]).then_inc(const, 16)
            sp.dma_start(mask[:], a["mask"].rearrange("d p n -> p d n")).then_inc(const, 16)
            sp.wait_ge(ready, 2)

            def load(d, p, c, with_q):
                rows = bass.ds(c * P, P)
                sp.dma_start(kb[:, d, p, :], s["proj1"][rows, C1_K:C1_K + D]).then_inc(ld[d][p], 16)
                sp.dma_start(vb[:, d, p, :, 0:MD], s["proj1"][rows, C1_V:C1_V + D].rearrange("p (h n) -> p h n", n=MD)).then_inc(ld[d][p], 16)
                if with_q:
                    sp.dma_start(qb[:, d, p, :], s["proj1"][rows, C1_Q:C1_Q + D]).then_inc(ld[d][p], 16)

            for p in range(2):
                for d in range(2):
                    load(d, p, ctx_chunk(p, d), False)
            with sp.Fori(0, TURNS) as v:
                for p in range(2):
                    for d in range(2):
                        sp.wait_ge(up_done, NU * v + p * 2 * MH + (d + 1) * MH)
                        load(d, p, chunk(v, p, d), True)

        @block.gpsimd
        def _(pool):
            nc.gpsimd.memset(vb[:, :, :, :, MD:MD + 1], 1.0).then_inc(ready, 1)
            nc.gpsimd.memset(vb[:, :, :, :, MD + 1:VC], 0.0).then_inc(ready, 1)

            def weighted(u, base, ldv, cv):
                p, d, hh = U[u]
                pool.wait_ge(ld[d][p], ldv)
                pool.wait_ge(col_done, cv + 2 * (p * 2 + d) + 2)
                wait(pool, up_mm, base, u - 1)
                nc.gpsimd.tensor_tensor(vw[:, u % 2, :], vb[:, d, p, hh, :], ccol[:, p, d, 0, 2 + d, hh:hh + 1].broadcast_to([P, VC]), ALU.mult).then_inc(vw_done, 1)

            def store(v, p, d):
                pool.wait_ge(h_done, NU * v + (p * 2 + d + 1) * MH)
                pool.dma_start(s["h"][d, bass.ds((chunk(v, p, d) - CT) * P, P), :], h[:, d, p, :]).then_inc(stored[d][p], 16)

            for u in range(NU):
                weighted(u, 0, 32, 0)
            with pool.Fori(0, TURNS) as v:
                pool.wait_ge(up_mm, NU * v + NU)
                for u in range(NU):
                    weighted(u, NU * v + NU, 48 * v + 80, 8 * v + 8)
                    if u % MH == MH - 1 and u > MH:
                        store(v, *divmod(u // MH - 1, 2))
                store(v, 1, 1)
            for d in range(2):
                for p in range(2):
                    pool.wait_ge(stored[d][p], 16 * TURNS)

        @block.scalar
        def _(act):
            with act.Fori(0, TURNS) as v:
                b = NU * v

                def evacuate(u):
                    act.wait_ge(tr_done, b + u + 1)
                    act.wait_ge(st_mm, b + max(u - 1, 0))
                    nc.scalar.activation(qkt[:, u % 2], tp[u % 2][:].rearrange("p (k n) -> p k n", n=P), ACT.Copy).then_inc(tr_out, 1)

                def decays(u):
                    p, d, hh = U[u]
                    act.wait_ge(mx_mm, b + u + 1)
                    act.wait_ge(col_done, 8 * v + 8 + 2 * (p * 2 + d) + 2)
                    act.wait_ge(sw_done, b + max(u - 1, 0))
                    nc.scalar.activation(dw[:, u % 2, :], pmx[:, 0:P], ACT.Exp, bias=ccol[:, p, d, 0, d, hh:hh + 1], scale=-1.0).then_inc(dw_done, 1)

                def from_state(u):
                    p, d, hh = U[u]
                    act.wait_ge(st_mm, b + u + 1)
                    act.wait_ge(total_done, b + max(u - 1, 0))
                    nc.scalar.activation(inter[:, u % 2, :], pst[:, 0:VC], ACT.Copy, scale=ccol[:, p, d, 1, d, hh:hh + 1]).then_inc(inter_done, 1)

                evacuate(0)
                for u in range(NU):
                    if u + 1 < NU:
                        evacuate(u + 1)
                    decays(u)
                    if u:
                        from_state(u - 1)
                from_state(NU - 1)

        @block.vector
        def _(dve):
            V = nc.vector
            V.memset(state[:], 0.0).then_inc(up_half, 1)

            def columns(p, d, c, seen):
                dve.wait_ge(up_done, seen)
                V.tensor_copy(ccol[:, p, d], cols[:, c]).then_inc(col_done, 1)
                V.tensor_copy(dcol[:, p, d, :], dec[:, :, c]).then_inc(col_done, 1)

            def update(u, base, cv):
                p, d, hh = U[u]
                dve.wait_ge(up_mm, base + u + 1)
                dve.wait_ge(col_done, cv + 2 * (p * 2 + d) + 2)
                dve.wait_ge(up_half, base + u + 1)
                for k, sem in enumerate((up_half, up_done)):
                    V.scalar_tensor_tensor(state[:, d, hh, k, :], state[:, d, hh, k, :], dcol[:, p, d, d * MH + hh:d * MH + hh + 1], pup[:, k, 0:VC], ALU.mult, ALU.add).then_inc(sem, 1)

            for p in range(2):
                for d in range(2):
                    columns(p, d, ctx_chunk(p, d), 0)
            for u in range(NU):
                update(u, 0, 0)
            with dve.Fori(0, TURNS) as v:
                b = NU * v
                for p in range(2):
                    for d in range(2):
                        columns(p, d, chunk(v, p, d), b + NU)

                def weights(u):
                    dve.wait_ge(sc_mm, b + u + 1)
                    dve.wait_ge(dw_done, b + u + 1)
                    dve.wait_ge(in_mm, b + max(u - 1, 0))
                    V.scalar_tensor_tensor(sw[:, u % 2, :], psc[:, 0:P], float(MD) ** -0.5, dw[:, u % 2, :], ALU.mult, ALU.mult).then_inc(sw_done, 1)

                def outputs(u):
                    p, d, hh = U[u]
                    dve.wait_ge(in_mm, b + u + 1)
                    dve.wait_ge(inter_done, b + u + 1)
                    dve.wait_ge(h_done, b + max(u - 1, 0))
                    V.tensor_tensor(total[:, u % 2, :], pin[:, 0:VC], inter[:, u % 2, :], ALU.add).then_inc(total_done, 1)
                    dve.wait_ge(total_done, b + u + 1)
                    c = Steps(dve, den_done, 3 * (b + u))
                    x = total[:, u % 2, MD:MD + 1]
                    c.did(V.scalar_tensor_tensor(den[:, 0:1], x, -1.0, x, ALU.mult, ALU.max))
                    c.wait()
                    c.did(V.tensor_tensor(den[:, 1:2], den[:, 0:1], ccol[:, p, d, 1, 2 + d, hh:hh + 1], ALU.max))
                    c.wait()
                    c.did(V.reciprocal(den[:, 2:3], den[:, 1:2]))
                    c.wait()
                    if hh == 0:
                        dve.wait_ge(stored[d][p], 16 * v)
                    V.tensor_scalar(h[:, d, p, hh * MD:(hh + 1) * MD], total[:, u % 2, 0:MD], den[:, 2:3], None, ALU.mult).then_inc(h_done, 1)

                for u in range(NU):
                    weights(u)
                    if u:
                        outputs(u - 1)
                        update(u - 1, b + NU, 8 * v + 8)
                outputs(NU - 1)
                update(NU - 1, b + NU, 8 * v + 8)

        @block.tensor
        def _(pe):
            mm = nc.tensor.matmul

            def update(u, base):
                p, d, hh = U[u]
                pe.wait_ge(vw_done, base + u + 1)
                pe.wait_ge(up_done, base + u)
                for k in range(2):
                    x = mm(pup[:, k, 0:VC], kb[:, d, p, hh * MD + k * P:hh * MD + (k + 1) * P], vw[:, u % 2, :], start=True, stop=True)
                x.then_inc(up_mm, 1)

            for u in range(NU):
                update(u, 0)
            pe.wait_ge(const, 32)
            with pe.Fori(0, TURNS) as v:
                b = NU * v

                def turned(u):
                    p, d, hh = U[u]
                    pe.wait_ge(ld[d][p], 48 * v + 80)
                    pe.wait_ge(tr_out, b + max(u - 1, 0))
                    for k, src in enumerate((qb, qb, kb, kb)):
                        x = nc.tensor.transpose(tp[u % 2][:, k * P:(k + 1) * P], src[:, d, p, hh * MD + (k % 2) * P:hh * MD + (k % 2 + 1) * P], keep["ident"][:])
                    x.then_inc(tr_done, 1)

                def scores(u):
                    p, d, hh = U[u]
                    pe.wait_ge(tr_out, b + u + 1)
                    pe.wait_ge(sw_done, b + u)
                    for k in range(2):
                        x = mm(psc[:, 0:P], qkt[:, u % 2, 2 + k, :], qkt[:, u % 2, k, :], start=(k == 0), stop=(k == 1))
                    x.then_inc(sc_mm, 1)
                    pe.wait_ge(dw_done, b + u)
                    mm(pmx[:, 0:P], sel[:, d * MH + hh, :], mrow[:, bass.ds(chunk(v, p, d) * P, P)], start=True, stop=False)
                    mm(pmx[:, 0:P], keep["ident"][:], mask[:, d, :], start=False, stop=True).then_inc(mx_mm, 1)

                def outputs(u):
                    p, d, hh = U[u]
                    pe.wait_ge(sw_done, b + u + 1)
                    pe.wait_ge(total_done, b + u)
                    mm(pin[:, 0:VC], sw[:, u % 2, :], vb[:, d, p, hh, :], start=True, stop=True).then_inc(in_mm, 1)
                    pe.wait_ge(inter_done, b + u)
                    pe.wait_ge(up_done, b + NU + max(u - 2 * MH + 1, 0) if u >= 2 * MH else b + u + 2 * MH + 1)
                    for k in range(2):
                        x = mm(pst[:, 0:VC], qkt[:, u % 2, k, :], state[:, d, hh, k, :], start=(k == 0), stop=(k == 1))
                    x.then_inc(st_mm, 1)

                turned(0)
                for u in range(NU):
                    if u + 1 < NU:
                        turned(u + 1)
                    scores(u)
                    if u:
                        outputs(u - 1)
                        update(u - 1, b + NU)
                outputs(NU - 1)
                update(NU - 1, b + NU)


def laid_out(x, c, ctx, c_ctx, ada_w, ada_b, post_ln_gain, post_ln_bias, even_w_in, even_q_gain, even_k_gain,
             even_f_gain, even_w_fmix, even_w_out, odd_w_in, odd_gate_bias, odd_w_out):
    a = {}
    a["x"] = np.concatenate([ctx[0], x[0]], 0)
    a["c_cols"] = np.stack([c[0].reshape(KD, P).T, c_ctx.reshape(KD, P).T], -1)
    a["ada_w"] = ada_w
    a["ada_b"] = ada_b
    a["ada_b_cols"] = ada_b[:, :2 * D].reshape(2, 16, P).transpose(2, 0, 1)
    a["post_gain"], a["post_bias"] = post_ln_gain, post_ln_bias
    w = even_w_in[0]
    q, ga, k, v, u, gb = np.split(w, np.cumsum([QW, QW, KVW, KVW, FW])[:5], axis=1)
    a["w0"] = np.concatenate([q, k, v, u, ga, gb], 1)
    a["qk_gain"] = np.concatenate([even_q_gain] * NQ + [even_k_gain] * NKV, 1)
    a["f_gain"] = even_f_gain.reshape(1, FW)
    mix = np.zeros((2, P, P), even_w_fmix.dtype)
    for g in range(4):
        o = (g % 2) * HD
        mix[g // 2, o:o + HD, o:o + HD] = even_w_fmix[0, g]
    a["fmix"] = mix
    a["w_out0"], a["w_out1"] = even_w_out[0], odd_w_out[0]
    w = odd_w_in[0]
    a["w1"] = np.concatenate([w[:, D:3 * D], w[:, 0:D], w[:, 3 * D:5 * D]], 1)
    wg = np.zeros((D, P), w.dtype)
    gb = np.zeros((P, 1), odd_gate_bias.dtype)
    for kind, row in ((0, 0), (1, 64), (2, 32), (3, 96)):
        wg[:, row:row + MH] = w[:, 5 * D + kind * MH:5 * D + (kind + 1) * MH]
        gb[row:row + MH, 0] = odd_gate_bias[0, kind * MH:(kind + 1) * MH]
    a["w_gate"], a["gate_bias"] = wg, gb
    return {n: np.ascontiguousarray(np.asarray(v)) for n, v in a.items()}


def tables():
    t = {"ident": np.eye(P)}
    t["fold"] = np.concatenate([np.concatenate([np.eye(HD)] * 2), np.zeros((P, P - HD))], 1)
    inv = 10000.0 ** -(np.arange(16, dtype=np.float32) / np.float32(16))
    inv = inv.astype(np.float32)
    n = np.arange(SEQ)
    ang = np.concatenate([(n // GRID_W).astype(np.float32)[:, None] * inv, (n % GRID_W).astype(np.float32)[:, None] * inv], 1)
    rope = np.zeros((T, 2, 32))
    rope[:CTX, 0] = 1.0
    rope[CTX:, 0], rope[CTX:, 1] = np.cos(ang.astype(np.float64)), np.sin(ang.astype(np.float64))
    t["rope"] = rope
    for name, length in (("dft_lat", SEQ), ("dft_ctx", CTX)):
        R = length // P
        p, r, mm = np.arange(P)[:, None, None], np.arange(R)[None, :, None], np.arange(P)[None, None, :]
        ang = 2 * np.pi * ((p * (R * mm + r)) % length) / length
        t[name] = np.stack([np.cos(ang), np.sin(ang)], 1) / np.sqrt(length * HD)
    j = np.arange(HD)
    ang = 2 * np.pi * (np.outer(j, j) % HD) / HD
    t["dft_head"] = np.stack([np.kron(np.eye(2), np.cos(ang)), np.kron(np.eye(2), -np.sin(ang))])
    s, q = np.arange(P)[:, None], np.arange(P)[None, :]
    t["mask"] = np.stack([np.where(s <= q, 0.0, MASKED), np.where(s >= q, 0.0, MASKED)])
    sel = np.zeros((P, 2 * MH, P))
    for d in range(2):
        for h in range(MH):
            sel[DIR_ROW[d] + h, d * MH + h] = 1.0
    t["sel"] = sel
    return {k: np.ascontiguousarray(v.astype(np.float32)) for k, v in t.items()}


def program(nc, a, out):
    m = Memory(nc)
    dram = lambda name, shape: nc.dram_tensor(name, list(shape), F32, kind="Internal").ap()
    s = {
        "gates": dram("s_gates", (3, P, D)),
        "proj0": dram("s_proj0", (T, W0_COLS)),
        "un": dram("s_un", (T, FW)),
        "q": dram("s_q", (NQ, NT, P, P)),
        "attn": dram("s_attn", (T, QW)),
        "four": dram("s_four", (T, FW)),
        "x1": dram("s_x1", (T, D)),
        "proj1": dram("s_proj1", (T, W1_COLS)),
        "h": dram("s_h", (2, SEQ, D)),
    }
    keep = {}
    for name, shape in (("mod", [P, 2, 2, NT, KD]), ("ident", [P, P])):
        keep[name] = m.all.enter_context(nc.sbuf_tensor("keep_" + name, shape, F32))
    setup = m.sem("ident_ld")
    with nc.Block() as block:

        @block.sync
        def _(sp):
            sp.dma_start(keep["ident"][:], a["ident"]).then_inc(setup, 16)
            sp.wait_ge(setup, 16)

    modulation(nc, m, a, s, keep)
    projections(nc, m, a, s, keep, 0, None)

    kres, vres = m.sb("kres", [P, 2 * NKV, T], F32R), m.sb("vres", [P, NT, NKV, P], F32R)
    attention_stack, m.stack = m.stack, ExitStack()
    heads(nc, m, a, s, keep, kres, vres)
    m.end()
    attention(nc, m, a, s, keep, kres, vres, "ac_", 0, CT, CT)
    m.end()
    attention(nc, m, a, s, keep, kres, vres, "al_", CT, LT, NT)
    m.end()
    attention_stack.close()
    fourier(nc, m, a, s, keep)
    m.end()
    mixer_out(nc, m, a, s, keep, 0, s["x1"])

    graw = m.sb("graw", [P, T])
    gates_stack, m.stack = m.stack, ExitStack()
    projections(nc, m, a, s, keep, 1, graw)
    mrow, cols, dec = m.sb("mrow", [P, T]), m.sb("cols", [P, NT, 2, 4, MH]), m.sb("dec", [P, 2 * MH, NT])
    scan_stack, m.stack = m.stack, ExitStack()
    gate_rows(nc, m, a, keep, graw, mrow, cols, dec)
    m.end()
    mlstm(nc, m, a, s, keep, mrow, cols, dec)
    m.end()
    scan_stack.close()
    gates_stack.close()
    mixer_out(nc, m, a, s, keep, 1, out[0])
    m.all.close()


def kernel(**inputs):
    from concourse import bacc
    from concourse.bass_utils import run_bass_kernel_spmd

    arrays = {**laid_out(**inputs), **tables()}
    nc = bacc.Bacc("TRN2", target_bir_lowering=False, num_devices=1)
    feed = {f"in_{n}": v for n, v in arrays.items()}
    aps = {n: nc.dram_tensor(f"in_{n}", v.shape, mybir.dt.from_np(v.dtype), kind="ExternalInput").ap() for n, v in arrays.items()}
    out = nc.dram_tensor("out_0", (1, SEQ, D), F32, kind="ExternalOutput").ap()
    program(nc, aps, out)
    r = run_bass_kernel_spmd(nc, [feed], core_ids=[0])
    return r.results[0]["out_0"]
```

```python
from contextlib import ExitStack

import numpy as np

import concourse.bass as bass
from concourse import mybir

F32 = mybir.dt.float32
F32R = mybir.dt.float32r
ALU = mybir.AluOpType
ACT = mybir.ActivationFunctionType
AX = mybir.AxisListType

P = 128
D = 1024
KD = D // P
SEQ, CTX = 2048, 256
T = SEQ + CTX
NT = T // P
CT = CTX // P
LT = SEQ // P
GRID_W = 64
HD = 64
NQ, NKV = 12, 4
QPK = NQ // NKV
QW, KVW, FW = NQ * HD, NKV * HD, 256
MH, MD = 4, 256
W0_COLS = 2560
W1_COLS = 5 * D
CH = 512
EPS = 1e-6
ALPHA = 4.0 ** 0.25
MASKED = 1e30
C_QK, C_V, C_U, C_GATE = 0, QW + KVW, QW + 2 * KVW, QW + 2 * KVW + FW
C1_K, C1_V, C1_Q, C1_O, C1_Z = (i * D for i in range(5))
NR = 36
DIR_ROW = (0, 32)
PARTS = ((0, 10), (10, 8))


class Memory:

    def __init__(self, nc):
        self.nc, self.stack, self.all, self.sems = nc, ExitStack(), ExitStack(), []

    def sb(self, name, shape, dt=F32):
        return self.stack.enter_context(self.nc.sbuf_tensor(name, shape, dt))

    def ps(self, name, shape=(P, 512)):
        return self.stack.enter_context(self.nc.psum_tensor(name, list(shape), F32))

    def sem(self, name, count=None):
        new = [self.nc.alloc_semaphore(name if count is None else f"{name}{i}") for i in range(count or 1)]
        self.sems += new
        return new[0] if count is None else new

    def free(self):
        self.stack.close()
        self.stack = ExitStack()

    def end(self):
        self.stack.close()
        self.stack = ExitStack()
        if self.sems:
            self.nc.all_engine_barrier()
            self.nc.clear_and_free_semaphores(self.sems)
            self.nc.all_engine_barrier()
            self.sems = []


class Steps:

    def __init__(self, eng, sem, base=0):
        self.eng, self.sem, self.base, self.n = eng, sem, base, 0

    def did(self, ins):
        ins.then_inc(self.sem, 1)
        self.n += 1

    def wait(self):
        self.eng.wait_ge(self.sem, self.base + self.n)


def modulation(nc, m, a, s, keep):
    ct = m.sb("mod_c", [P, KD, 2])
    sil = m.sb("mod_silu", [P, KD, 2])
    sil_row = m.sb("mod_silu_row", [P, 2, KD, P])
    wbuf = m.sb("mod_w", [P, 2, KD, CH])
    bcol = m.sb("mod_bcol", [P, 2, 16])
    brow = m.sb("mod_brow", [P, 2, D])
    cols = m.sb("mod_cols", [P, 2, 16, 2])
    gate = m.sb("mod_gate", [P, 6, CH])
    pcol = m.ps("mod_pcol")
    prow = [m.ps(f"mod_prow{i}") for i in range(2)]
    small = m.sem("mod_small")
    silu_done, rows_done = m.sem("mod_silu_done"), m.sem("mod_rows_done")
    w_ld = m.sem("mod_w_ld", 2)
    col_mm, col_done = m.sem("mod_col_mm"), m.sem("mod_col_done")
    row_mm, row_done = m.sem("mod_row_mm"), m.sem("mod_row_done")
    st = m.sem("mod_store")
    NCH = 6
    rows = [(l, src, h) for l in range(2) for h in range(2) for src in range(2) if (l, src) != (1, 1)]
    used, n_col, n_row = [], 0, 0
    for n in range(2 * NCH):
        if n % NCH < 4:
            n_col += 1
            used.append((col_mm, n_col))
        else:
            n_row += 2 if n < NCH else 1
            used.append((row_mm, n_row))
    PER_LAYER = 6
    with nc.Block() as block:

        @block.sync
        def _(sp):
            sp.dma_start(ct[:], a["c_cols"]).then_inc(small, 16)
            sp.dma_start(bcol[:], a["ada_b_cols"]).then_inc(small, 16)
            for l in range(2):
                sp.dma_start(brow[:, l, :], a["ada_b"][l:l + 1, 2 * D:3 * D].broadcast_to([P, D])).then_inc(small, 16)
            for n in range(2 * NCH):
                l, c = n // NCH, n % NCH
                if n >= 2:
                    sp.wait_ge(*used[n - 2])
                sp.dma_start(wbuf[:, n % 2], a["ada_w"][l, :, c * CH:(c + 1) * CH].rearrange("(k p) n -> p k n", p=P)).then_inc(w_ld[n % 2], 16)

        @block.scalar
        def _(act):
            act.wait_ge(small, 64)
            nc.scalar.activation(sil[:], ct[:], ACT.Silu).then_inc(silu_done, 1)
            for n, (l, src, h) in enumerate(rows):
                act.wait_ge(row_done, n + 1)
                act.dma_start(s["gates"][l * 2 + src, :, h * CH:(h + 1) * CH], gate[:, n, :]).then_inc(st, 16)
            act.wait_ge(st, 16 * len(rows))

        @block.vector
        def _(dve):
            dve.wait_ge(silu_done, 1)
            for src in range(2):
                nc.vector.tensor_copy(sil_row[:, src], sil[:, :, src:src + 1].broadcast_to([P, KD, P])).then_inc(rows_done, 1)
            nr = 0
            for l in range(2):
                dve.wait_ge(*used[l * NCH + 3])
                nc.vector.tensor_tensor(cols[:, l], pcol[:, 0:32].rearrange("p (t s) -> p t s", s=2),
                                        bcol[:, l, :].unsqueeze(2).broadcast_to([P, 16, 2]), ALU.add).then_inc(col_done, 1)
                dve.wait_ge(col_done, PER_LAYER * l + 1)
                nc.vector.tensor_scalar(cols[:, l, 8:16], cols[:, l, 8:16], 1.0, None, ALU.add).then_inc(col_done, 1)
                dve.wait_ge(col_done, PER_LAYER * l + 2)
                for which in range(2):
                    v = cols[:, l, 8 * which:8 * which + 8, :]
                    nc.vector.tensor_copy(keep["mod"][:, l, which, CT:NT, :], v[:, :, 0].unsqueeze(1).broadcast_to([P, LT, KD])).then_inc(col_done, 1)
                    nc.vector.tensor_copy(keep["mod"][:, l, which, 0:CT, :], v[:, :, 1].unsqueeze(1).broadcast_to([P, CT, KD])).then_inc(col_done, 1)
                for h in range(2):
                    for src in range(2 - l):
                        dve.wait_ge(row_mm, nr + 1)
                        nc.vector.tensor_tensor(gate[:, nr, :], prow[nr % 2][:], brow[:, l, h * CH:(h + 1) * CH], ALU.add).then_inc(row_done, 1)
                        nr += 1

        @block.tensor
        def _(pe):
            pe.wait_ge(rows_done, 2)
            nr = 0
            for n in range(2 * NCH):
                l, c = n // NCH, n % NCH
                pe.wait_ge(w_ld[n % 2], 16 * (n // 2 + 1))
                if c < 4:
                    if l == 1 and c == 0:
                        pe.wait_ge(col_done, 1)
                    for j in range(4):
                        t = 4 * c + j
                        for k in range(KD):
                            mm = nc.tensor.matmul(pcol[:, 2 * t:2 * t + 2], wbuf[:, n % 2, k, j * P:(j + 1) * P], sil[:, k, :],
                                                  start=(k == 0), stop=(k == KD - 1))
                    mm.then_inc(col_mm, 1)
                else:
                    for src in range(2 - l):
                        if nr >= 2:
                            pe.wait_ge(row_done, nr - 1)
                        for k in range(KD):
                            mm = nc.tensor.matmul(prow[nr % 2][:], sil_row[:, src, k, :], wbuf[:, n % 2, k, :], start=(k == 0), stop=(k == KD - 1))
                        mm.then_inc(row_mm, 1)
                        nr += 1
    m.end()


def normalised(nc, m, layer, x_src, mod, h_hi, h_lo, first, count, ident, w_src, wbuf):
    wst, whi, wlo = wbuf
    tag = f"ln{layer}{first}_"
    x = m.sb(tag + "x", [P, 2, D])
    xn = m.sb(tag + "xn", [P, 2, D])
    hf = m.sb(tag + "h", [P, 2, KD, P])
    stats = m.sb(tag + "stats", [P, 2, 2, 6])
    mv = m.sb(tag + "mv", [P, 2, 2])
    rstd = m.sb(tag + "rstd", [P, 2, 1])
    mcol = m.sb(tag + "mcol", [P, 2, 2, KD])
    half, eps, warm = m.sb(tag + "half", [P, 1]), m.sb(tag + "eps", [P, 1]), m.sb(tag + "warm", [P, 1])
    first_w, first_w_hi, first_w_lo = (m.sem(tag + "first_w" + x) for x in ("", "_hi", "_lo"))
    HALF, PIECE = count // 2 - 2, KD // 2
    hf2_done, warm_done = m.sem(tag + "hf2", 2), m.sem(tag + "warm_done")
    tp = [m.ps(tag + f"tp{i}", (P, 2, 512)) for i in range(2)]
    x_ld, x_used = m.sem(tag + "x_ld", 2), m.sem(tag + "x_used", 2)
    stats_done, mcol_done, var_done, rstd_done = m.sem(tag + "stats"), m.sem(tag + "mcol"), m.sem(tag + "var"), m.sem(tag + "rstd_done")
    tr_done, hf_done = m.sem(tag + "tr", 2), m.sem(tag + "hf", 2)
    hi_done, lo_done, ready = m.sem(tag + "hi", 2), m.sem(tag + "lo", 2), m.sem(tag + "ready")
    with nc.Block() as block:

        @block.sync
        def _(sp):
            with sp.Fori(0, count // 2) as v:
                for p in range(2):
                    sp.wait_ge(x_used[p], v)
                    sp.dma_start(x[:, p, :], x_src[bass.ds((2 * v + p + first) * P, P), :]).then_inc(x_ld[p], 16)

        @block.vector
        def _(dve):
            def statistics(n, p, v):
                dve.wait_ge(x_ld[p], 16 * v + 16)
                for h in range(2):
                    nc.vector.bn_stats(stats[:, p, h, :], x[:, p, h * 512:(h + 1) * 512]).then_inc(stats_done, 1)
                dve.wait_ge(stats_done, 2 * n + 2)
                if not (isinstance(n, int) and n < 2):
                    dve.wait_ge(hf2_done[p], v)
                nc.vector.tensor_copy(mcol[:, p], mod[:, layer, :, n + first, :]).then_inc(mcol_done, 1)
                nc.vector.bn_aggr(mv[:, p, :], stats[:, p].rearrange("p a b -> p (a b)")).then_inc(var_done, 1)

            def normalise(n, p, v):
                dve.wait_ge(rstd_done, n + 1)
                dve.wait_ge(tr_done[p], v)
                nc.vector.tensor_scalar(xn[:, p, :], x[:, p, :], mv[:, p, 0:1], rstd[:, p, :], ALU.subtract, ALU.mult).then_inc(x_used[p], 1)

            def modulate(n, p, v):
                dve.wait_ge(mcol_done, n + 1)
                dve.wait_ge(tr_done[p], v + 1)
                dve.wait_ge(lo_done[p], v)
                for k in range(KD // 2):
                    ins = nc.vector.tensor_scalar(hf[:, p, k, :], tp[p][:, k // 4, (k % 4) * P:(k % 4 + 1) * P],
                                                  mcol[:, p, 1, k:k + 1], mcol[:, p, 0, k:k + 1], ALU.mult, ALU.add)
                ins.then_inc(hf_done[p], 1)

            def body(n, p, v):
                statistics(n + 1, 1 - p, v + p)
                modulate(n, p, v)
                normalise(n + 1, 1 - p, v + p)

            statistics(0, 0, 0)
            normalise(0, 0, 0)
            with dve.Fori(0, HALF) as v:
                for p in range(2):
                    body(2 * v + p, p, v)

            def weights_low(i):
                part = slice(i * PIECE, (i + 1) * PIECE)
                dve.wait_ge(first_w_hi, i + 1)
                nc.vector.tensor_tensor(wlo[:, 0, part], wst[:, part], whi[:, 0, part].bitcast(F32), ALU.subtract).then_inc(first_w_lo, 1)

            for n in range(2 * HALF, count - 1):
                body(n, n % 2, n // 2)
                if n % 2:
                    weights_low(n // 2 - HALF)
            modulate(count - 1, 1, count // 2 - 1)
            weights_low(1)

        @block.gpsimd
        def _(pool):
            nc.gpsimd.memset(half[:], -0.5).then_inc(ready, 1)
            nc.gpsimd.memset(eps[:], EPS).then_inc(ready, 1)
            pool.wait_ge(ready, 2)

            def inverse_deviation(n, p):
                pool.wait_ge(var_done, n + 1)
                nc.gpsimd.tensor_tensor(rstd[:, p, :], mv[:, p, 1:2], eps[:], ALU.add).then_inc(ready, 1)
                pool.wait_ge(ready, n + 3)
                nc.gpsimd.tensor_tensor(rstd[:, p, :], rstd[:, p, :], half[:], ALU.pow).then_inc(rstd_done, 1)

            def low_part(n, p, v):
                pool.wait_ge(hi_done[p], v + 1)
                nc.gpsimd.tensor_tensor(h_lo[:, :, n, :], hf[:, p], h_hi[:, :, n, :].bitcast(F32), ALU.subtract).then_inc(lo_done[p], 1)

            inverse_deviation(0, 0)
            inverse_deviation(1, 1)
            with pool.Fori(0, count // 2 - 1) as v:
                for p in range(2):
                    inverse_deviation(2 * v + p + 2, p)
                    low_part(2 * v + p, p, v)
            for p in range(2):
                low_part(count - 2 + p, p, count // 2 - 1)

        @block.scalar
        def _(act):
            act.wait_ge(ready, 1)
            nc.scalar.activation(warm[:], half[:], ACT.Identity).then_inc(warm_done, 1)
            act.wait_ge(x_ld[1], 16)
            act.dma_start(wst[:], w_src[:, 0:CH].rearrange("(k p) n -> p k n", p=P)).then_inc(first_w, 16)

            def body(n, p, v):
                act.wait_ge(mcol_done, n + 1)
                act.wait_ge(tr_done[p], v + 1)
                act.wait_ge(lo_done[p], v)
                for k in range(KD // 2, KD):
                    ins = nc.scalar.activation(hf[:, p, k, :], tp[p][:, k // 4, (k % 4) * P:(k % 4 + 1) * P],
                                               ACT.Identity, bias=mcol[:, p, 0, k:k + 1], scale=mcol[:, p, 1, k:k + 1])
                ins.then_inc(hf2_done[p], 1)
                act.wait_ge(hf_done[p], v + 1)
                act.wait_ge(hf2_done[p], v + 1)
                nc.scalar.activation(h_hi[:, :, n, :], hf[:, p], ACT.Copy).then_inc(hi_done[p], 1)

            with act.Fori(0, HALF) as v:
                for p in range(2):
                    body(2 * v + p, p, v)
            act.wait_ge(first_w, 16)
            for n in range(2 * HALF, count):
                body(n, n % 2, n // 2)
                if n % 2 == 0:
                    part = slice((n // 2 - HALF) * PIECE, (n // 2 - HALF + 1) * PIECE)
                    nc.scalar.activation(whi[:, 0, part], wst[:, part], ACT.Copy).then_inc(first_w_hi, 1)

        @block.tensor
        def _(pe):
            with pe.Fori(0, count // 2) as v:
                for p in range(2):
                    pe.wait_ge(x_used[p], v + 1)
                    pe.wait_ge(hf_done[p], v)
                    pe.wait_ge(hf2_done[p], v)
                    for k in range(KD):
                        tr = nc.tensor.transpose(tp[p][:, k // 4, (k % 4) * P:(k % 4 + 1) * P], xn[:, p, k * P:(k + 1) * P], ident[:])
                    tr.then_inc(tr_done[p], 1)


def split_mm(nc, out, s_hi, s_lo, m_hi, m_lo, start, stop):
    nc.tensor.matmul(out, s_hi, m_hi, start=start, stop=False)
    nc.tensor.matmul(out, s_hi, m_lo, start=False, stop=False)
    return nc.tensor.matmul(out, s_lo, m_hi, start=False, stop=stop)


def projected(nc, m, tag, w_src, out, h_hi, h_lo, wbuf, chunks, first, tiles, gates=None, ahead=0):
    wst, whi, wlo = wbuf
    nt = len(tiles)
    NS = nt // 2
    stage = m.sb(tag + "stage", [P, NS, CH])
    acc = [m.ps(tag + f"acc{i}") for i in range(NS)]
    w_ld, hi_done, lo_done = m.sem(tag + "w_ld"), m.sem(tag + "w_hi"), m.sem(tag + "w_lo")
    used = m.sem(tag + "w_used", 2)
    mm_done, out_done, stored = m.sem(tag + "mm", NS), m.sem(tag + "out", NS), m.sem(tag + "stored", NS)
    c0, nch = chunks[0], len(chunks)
    if gates is not None:
        wg, wg_hi, wg_lo, graw, gbias, wg_src, gbias_src = gates
        gacc = [m.ps(tag + f"gacc{i}") for i in range(2)]
        g_ld, g_split, g_mm, g_out = m.sem(tag + "g_ld"), m.sem(tag + "g_split"), m.sem(tag + "g_mm"), m.sem(tag + "g_out")
        spans = [(t0, min(4, nt - t0)) for t0 in range(0, nt, 4)]

    def over_chunks(eng, body):
        with eng.Fori(0, nch // 2) as v:
            for p in range(2):
                body(2 * v + p, v, p)
        if nch % 2:
            body(nch - 1, nch // 2, 0)

    def over_loads(eng, body):
        total = nch + ahead
        body(1, 0, 1)
        with eng.Fori(1, total // 2) as v:
            for p in range(2):
                body(2 * v + p, v, p)
        if total % 2:
            body(total - 1, total // 2, 0)

    with nc.Block() as block:

        @block.sync
        def _(sp):
            def store(c, v, p):
                for j in range(nt):
                    q = j % NS
                    sp.wait_ge(out_done[q], 2 * c + j // NS + 1)
                    sp.dma_start(out[(first + tiles[j]) * P:(first + tiles[j] + 1) * P, bass.ds((c + c0) * CH, CH)], stage[:, q, :]).then_inc(stored[q], 16)

            over_chunks(sp, store)
            for q in range(NS):
                sp.wait_ge(stored[q], 16 * 2 * nch)

        @block.scalar
        def _(act):
            if gates is not None:
                act.dma_start(wg[:], wg_src).then_inc(g_ld, 16)
                act.dma_start(gbias[:], gbias_src).then_inc(g_ld, 16)

            def load(c, v, p):
                act.wait_ge(lo_done, c - 1)
                act.dma_start(wst[:], w_src[:, bass.ds((c + c0) * CH, CH)].rearrange("(k p) n -> p k n", p=P)).then_inc(w_ld, 16)
                act.wait_ge(w_ld, 16 * c)
                act.wait_ge(used[p], v)
                nc.scalar.activation(whi[:, p], wst[:], ACT.Copy).then_inc(hi_done, 1)

            over_loads(act, load)

        @block.gpsimd
        def _(pool):
            def split(c, v, p):
                pool.wait_ge(w_ld, 16 * c)
                pool.wait_ge(hi_done, c)
                nc.gpsimd.tensor_tensor(wlo[:, p], wst[:], whi[:, p].bitcast(F32), ALU.subtract).then_inc(lo_done, 1)

            over_loads(pool, split)

        @block.vector
        def _(dve):
            if gates is not None:
                dve.wait_ge(g_ld, 32)
                nc.vector.tensor_copy(wg_hi[:], wg[:]).then_inc(g_split, 1)
                dve.wait_ge(g_split, 1)
                nc.vector.tensor_tensor(wg_lo[:], wg[:], wg_hi[:].bitcast(F32), ALU.subtract).then_inc(g_split, 1)
                for i, (t0, n) in enumerate(spans):
                    dve.wait_ge(g_mm, i + 1)
                    nc.vector.tensor_scalar(graw[:, (first + t0) * P:(first + t0 + n) * P], gacc[i % 2][:, 0:n * P], gbias[:], None, ALU.add).then_inc(g_out, 1)

            def out_of_psum(c, v, p):
                for j in range(nt):
                    q = j % NS
                    if j < nt - 1:
                        dve.wait_ge(mm_done[q], (2 if q < NS - 1 else 1) * c + j // NS + 1)
                    else:
                        dve.wait_ge(used[p], v + 1)
                    dve.wait_ge(stored[q], 16 * (2 * c + j // NS))
                    nc.vector.tensor_copy(stage[:, q, :], acc[q][:]).then_inc(out_done[q], 1)

            over_chunks(dve, out_of_psum)

        @block.tensor
        def _(pe):
            if gates is not None:
                pe.wait_ge(g_split, 2)
                for i, (t0, n) in enumerate(spans):
                    if i >= 2:
                        pe.wait_ge(g_out, i - 1)
                    for k in range(KD):
                        mm = split_mm(nc, gacc[i % 2][:, 0:n * P], wg_hi[:, k, :], wg_lo[:, k, :],
                                      h_hi[:, k, t0:t0 + n, :].rearrange("p t n -> p (t n)"), h_lo[:, k, t0:t0 + n, :].rearrange("p t n -> p (t n)"),
                                      k == 0, k == KD - 1)
                    mm.then_inc(g_mm, 1)

            def products(c, v, p):
                pe.wait_ge(lo_done, c)
                for j in range(nt):
                    q = j % NS
                    pe.wait_ge(out_done[q], 2 * c + j // NS)
                    for k in range(KD):
                        mm = split_mm(nc, acc[q][:], h_hi[:, k, tiles[j], :], h_lo[:, k, tiles[j], :], whi[:, p, k, :], wlo[:, p, k, :], k == 0, k == KD - 1)
                    mm.then_inc(mm_done[q] if j < nt - 1 else used[p], 1)

            over_chunks(pe, products)


def projections(nc, m, a, s, keep, layer, graw):
    ncols = (W0_COLS, W1_COLS)[layer]
    x_src, w_src, out = ((a["x"], a["w0"], s["proj0"]), (s["x1"], a["w1"], s["proj1"]))[layer]
    for part, (first, count) in enumerate(PARTS):
        tag = f"pj{layer}{part}_"
        h_hi = m.sb(tag + "h_hi", [P, KD, count, P], F32R)
        h_lo = m.sb(tag + "h_lo", [P, KD, count, P], F32R)
        wbuf = (m.sb(tag + "wst", [P, KD, CH]), m.sb(tag + "whi", [P, 2, KD, CH], F32R), m.sb(tag + "wlo", [P, 2, KD, CH], F32R))
        outer, m.stack = m.stack, ExitStack()
        normalised(nc, m, layer, x_src, keep["mod"], h_hi, h_lo, first, count, keep["ident"], w_src, wbuf)
        m.end()
        if layer == 0:
            projected(nc, m, tag, w_src, out, h_hi, h_lo, wbuf, range(ncols // CH), first, range(count))
        else:
            gates = (m.sb(tag + "wg", [P, KD, P]), m.sb(tag + "wg_hi", [P, KD, P], F32R), m.sb(tag + "wg_lo", [P, KD, P], F32R), graw,
                     m.sb(tag + "gbias", [P, 1]), a["w_gate"].rearrange("(k p) n -> p k n", p=P), a["gate_bias"])
            if part == 0:
                with_weights, m.stack = m.stack, ExitStack()
                projected(nc, m, tag, w_src, out, h_hi, h_lo, wbuf, range(0, 4), first, range(count), gates, 1)
                m.free()
                m.stack = with_weights
                projected(nc, m, tag + "b", w_src, out, h_hi, h_lo, wbuf, range(4, 10), first, range(CT, count))
            else:
                projected(nc, m, tag, w_src, out, h_hi, h_lo, wbuf, range(0, 10), first, range(count), gates)
        m.end()
        m.stack = outer
        m.end()


def wait(eng, sem, base, n):
    if not (isinstance(n, int) and n <= 0):
        eng.wait_ge(sem, base + n)


def over_turns(eng, count, before, body, after=None):
    before()
    for p in range(2):
        body(p, p, 0)
    with eng.Fori(1, count // 2 - 1) as v:
        for p in range(2):
            body(2 * v + p, p, v)
    for p in range(2):
        body(count - 2 + p, p, count // 2 - 1)
    if after:
        after()


def tile(fn, count, n, p, v, step):
    q = (p + step) % 2
    w = v + (p + step - q) // 2
    if not isinstance(n, int) or 0 <= n + step < count:
        fn(n + step, q, w)


def heads(nc, m, a, s, keep, kres, vres):
    NHD = NQ + NKV
    raw = m.sb("hd_raw", [P, 2, C_GATE])
    rope = m.sb("hd_rope", [P, 2, 2, 32])
    sq = m.sb("hd_sq", [P, C_GATE])
    ss = m.sb("hd_ss", [P, C_GATE // HD])
    rs = m.sb("hd_rs", [P, C_GATE // HD])
    nrm = m.sb("hd_nrm", [P, NHD, HD])
    un = m.sb("hd_un", [P, 2, FW])
    gq = m.sb("hd_gq", [P, D])
    gf = m.sb("hd_gf", [P, FW])
    half, eps = m.sb("hd_half", [P, C_GATE // HD]), m.sb("hd_eps", [P, C_GATE // HD])
    prod = m.sb("hd_prod", [P, 4, NHD, 32])
    rot = m.sb("hd_rot", [P, 2, NHD, HD])
    parts = m.sb("hd_parts", [P, NQ + 2 * NKV, P], F32R)
    qt = m.sb("hd_qt", [P, 2, NQ, P], F32R)
    NGR = (NQ + 2 * NKV) // 4
    tp = [m.ps(f"hd_tp{i}") for i in range(NGR)]
    const, ld = m.sem("hd_const"), m.sem("hd_ld", 2)
    raw_used, un_done = m.sem("hd_raw_used", 2), m.sem("hd_un_done", 2)
    vhi_done, un_half = m.sem("hd_vhi"), m.sem("hd_un_half")
    sq_done, ss_done, rs_done, ready = m.sem("hd_sq_done"), m.sem("hd_ss_done"), m.sem("hd_rs_done"), m.sem("hd_ready")
    chain, nrm_done, prod_done, rot_done = (m.sem("hd_" + x) for x in ("chain", "nrm_done", "prod_done", "rot_done"))
    hi_done, lo_done = m.sem("hd_hi_done"), m.sem("hd_lo_done")
    tr_done, tr_out, stored, un_stored = m.sem("hd_tr", NGR), m.sem("hd_tr_out", NGR), m.sem("hd_stored", 2), m.sem("hd_un_stored", 2)
    ident = keep["ident"]
    bq = C_QK + D
    with nc.Block() as block:

        @block.sync
        def _(sp):
            sp.dma_start(gq[:], a["qk_gain"].broadcast_to([P, D])).then_inc(const, 16)
            sp.dma_start(gf[:], a["f_gain"].broadcast_to([P, FW])).then_inc(const, 16)
            with sp.Fori(0, NT // 2) as v:
                for p in range(2):
                    t = 2 * v + p
                    sp.wait_ge(raw_used[p], v)
                    sp.wait_ge(un_done[p], v)
                    sp.dma_start(raw[:, p, :], s["proj0"][bass.ds(t * P, P), 0:C_GATE]).then_inc(ld[p], 16)
                    sp.dma_start(rope[:, p], a["rope"][bass.ds(t * P, P)]).then_inc(ld[p], 16)

        @block.scalar
        def _(act):
            def squares(n, p, v):
                act.wait_ge(ld[p], 32 * v + 32)
                act.wait_ge(ss_done, n)
                nc.scalar.activation(sq[:], raw[:, p, :], ACT.Square).then_inc(sq_done, 1)

            def values_high(n, p, v):
                nc.scalar.activation(vres[:, n, :, 0:HD], raw[:, p, C_V:C_U].rearrange("p (h d) -> p h d", d=HD), ACT.Copy).then_inc(vhi_done, 1)

            def high_part(n, p, v):
                for g in range(NGR):
                    act.wait_ge(tr_done[g], n)
                act.wait_ge(rot_done, n + 1)
                nc.scalar.activation(parts[:, 0:NHD, 0:HD], rot[:, p], ACT.Copy).then_inc(hi_done, 1)
                nc.scalar.activation(parts[:, NQ:NHD, HD:P], rot[:, p, NQ:NHD, :], ACT.Copy).then_inc(hi_done, 1)

            def out_of_psum(n, p, v):
                for g in range(NGR):
                    act.wait_ge(tr_done[g], n + 1)
                    if g == 0:
                        act.wait_ge(stored[p], 16 * v)
                    src = tp[g][:].rearrange("p (h n) -> p h n", n=P)
                    dst = qt[:, p, 4 * g:4 * g + 4, :] if g < 3 else kres[:, 4 * (g - 3):4 * (g - 3) + 4, bass.ds(n * P, P)]
                    nc.scalar.activation(dst, src, ACT.Copy).then_inc(tr_out[g], 1)
                for g in range(3):
                    act.wait_ge(tr_out[g], n + 1)
                act.dma_start(s["q"][:, n].rearrange("h p n -> p h n"), qt[:, p].bitcast(F32)).then_inc(stored[p], 16)
                act.wait_ge(un_done[p], v + 1)
                act.dma_start(s["un"][bass.ds(n * P, P), :], un[:, p, :]).then_inc(un_stored[p], 16)

            def before():
                squares(0, 0, 0)
                values_high(0, 0, 0)
                squares(1, 1, 0)

            def body(n, p, v):
                high_part(n, p, v)
                tile(squares, NT, n, p, v, 2)
                tile(values_high, NT, n, p, v, 1)
                out_of_psum(n, p, v)

            over_turns(act, NT, before, body)
            for p in range(2):
                act.wait_ge(stored[p], 16 * (NT // 2))
                act.wait_ge(un_stored[p], 16 * (NT // 2))

        @block.gpsimd
        def _(pool):
            nc.gpsimd.memset(half[:], -0.5).then_inc(ready, 1)
            nc.gpsimd.memset(eps[:], HD * EPS).then_inc(ready, 1)
            pool.wait_ge(ready, 2)
            pool.wait_ge(const, 34)
            with pool.Fori(0, NT // 2) as v:
                for p in range(2):
                    n = 2 * v + p
                    pool.wait_ge(ss_done, n + 1)
                    nc.gpsimd.tensor_tensor(rs[:], ss[:], eps[:], ALU.add).then_inc(ready, 1)
                    pool.wait_ge(ready, n + 3)
                    nc.gpsimd.tensor_tensor(rs[:], rs[:], half[:], ALU.pow).then_inc(rs_done, 1)
                    pool.wait_ge(rs_done, n + 1)
                    pool.wait_ge(un_stored[p], 16 * v)
                    nc.gpsimd.tensor_tensor(un[:, p].rearrange("p (h d) -> p h d", d=HD), raw[:, p, C_U:C_GATE].rearrange("p (h d) -> p h d", d=HD),
                                            rs[:, C_U // HD:].unsqueeze(2).broadcast_to([P, FW // HD, HD]), ALU.mult).then_inc(un_half, 1)
                    pool.wait_ge(nrm_done, n + 1)
                    pool.wait_ge(rot_done, n)
                    nc.gpsimd.tensor_tensor(prod[:, 2], nrm[:, :, 32:64], rope[:, p, 1, :].unsqueeze(1).broadcast_to([P, NHD, 32]), ALU.mult).then_inc(prod_done, 1)
                    nc.gpsimd.tensor_tensor(prod[:, 3], nrm[:, :, 32:64], rope[:, p, 0, :].unsqueeze(1).broadcast_to([P, NHD, 32]), ALU.mult).then_inc(prod_done, 1)
                    pool.wait_ge(un_half, n + 1)
                    nc.gpsimd.tensor_tensor(un[:, p], un[:, p], gf[:], ALU.mult).then_inc(un_done[p], 1)

        @block.vector
        def _(dve):
            dve.wait_ge(const, 32)
            nc.vector.tensor_scalar(gq[:, QW:], gq[:, QW:], float(HD) ** 0.5, None, ALU.mult).then_inc(const, 1)
            nc.vector.tensor_scalar(gf[:], gf[:], float(HD) ** 0.5, None, ALU.mult).then_inc(const, 1)
            dve.wait_ge(const, 34)
            K = 4

            def sums(n, p, v):
                dve.wait_ge(sq_done, n + 1)
                dve.wait_ge(rs_done, n)
                nc.vector.tensor_reduce(ss[:], sq[:].rearrange("p (h d) -> p h d", d=HD), AX.X, ALU.add).then_inc(ss_done, 1)

            def norms(n, p, v):
                c = Steps(dve, chain, n * K)
                dve.wait_ge(rs_done, n + 1)
                dve.wait_ge(prod_done, 2 * n)
                c.did(nc.vector.tensor_tensor(nrm[:], raw[:, p, 0:bq].rearrange("p (h d) -> p h d", d=HD), rs[:, 0:NHD].unsqueeze(2).broadcast_to([P, NHD, HD]), ALU.mult))
                c.wait()
                nc.vector.tensor_tensor(nrm[:], nrm[:], gq[:].rearrange("p (h d) -> p h d", d=HD), ALU.mult).then_inc(nrm_done, 1)
                dve.wait_ge(nrm_done, n + 1)
                for i in range(2):
                    c.did(nc.vector.tensor_tensor(prod[:, i], nrm[:, :, 0:32], rope[:, p, i, :].unsqueeze(1).broadcast_to([P, NHD, 32]), ALU.mult))

            def rotation(n, p, v):
                dve.wait_ge(chain, n * K + 3)
                dve.wait_ge(prod_done, 2 * n + 2)
                nc.vector.tensor_tensor(rot[:, p, :, 0:32], prod[:, 0], prod[:, 2], ALU.subtract).then_inc(chain, 1)
                nc.vector.tensor_tensor(rot[:, p, :, 32:64], prod[:, 1], prod[:, 3], ALU.add).then_inc(rot_done, 1)

            def low_part(n, p, v):
                dve.wait_ge(hi_done, 2 * n + 2)
                dve.wait_ge(rot_done, n + 1)
                nc.vector.tensor_tensor(parts[:, 0:NQ, HD:P], rot[:, p, 0:NQ, :], parts[:, 0:NQ, 0:HD].bitcast(F32), ALU.subtract).then_inc(lo_done, 1)
                for i in range(2):
                    nc.vector.tensor_tensor(parts[:, NHD:, i * HD:(i + 1) * HD], rot[:, p, NQ:NHD, :], parts[:, NQ:NHD, 0:HD].bitcast(F32), ALU.subtract).then_inc(lo_done, 1)

            def values_low(n, p, v):
                dve.wait_ge(vhi_done, n + 1)
                nc.vector.tensor_tensor(vres[:, n, :, HD:P], raw[:, p, C_V:C_U].rearrange("p (h d) -> p h d", d=HD), vres[:, n, :, 0:HD].bitcast(F32), ALU.subtract).then_inc(raw_used[p], 1)

            def before():
                sums(0, 0, 0)
                norms(0, 0, 0)
                values_low(0, 0, 0)

            def body(n, p, v):
                tile(sums, NT, n, p, v, 1)
                rotation(n, p, v)
                tile(norms, NT, n, p, v, 1)
                low_part(n, p, v)
                tile(values_low, NT, n, p, v, 1)

            over_turns(dve, NT, before, body)

        @block.tensor
        def _(pe):
            with pe.Fori(0, NT // 2) as v:
                for p in range(2):
                    n = 2 * v + p
                    pe.wait_ge(lo_done, 3 * n + 3)
                    for g in range(NGR):
                        pe.wait_ge(tr_out[g], n)
                        for i in range(4):
                            tr = nc.tensor.transpose(tp[g][:, i * P:(i + 1) * P], parts[:, 4 * g + i, :].bitcast(F32), ident[:])
                        tr.then_inc(tr_done[g], 1)


def attention(nc, m, a, s, keep, kres, vres, tag, q0, nq, nk):
    groups = [(4 * b, min(4, nk - 4 * b)) for b in range((nk + 3) // 4)]
    G, M = len(groups), QPK * nq
    V = M // 2
    q = m.sb(tag + "q", [P, 2, P], F32R)
    e = m.sb(tag + "e", [P, 2, nk * P])
    e_hi = m.sb(tag + "e_hi", [P, nk, 2, P], F32R)
    e_lo = m.sb(tag + "e_lo", [P, nk, 2, P], F32R)
    vcur = m.sb(tag + "vcur", [P, nk, P], F32R)
    mx = m.sb(tag + "mx", [P, G])
    nbias = m.sb(tag + "nbias", [P, 2])
    esum = m.sb(tag + "esum", [P, 2, G])
    tot = m.sb(tag + "tot", [P, 2])
    rden = m.sb(tag + "rden", [P, 2])
    ot = m.sb(tag + "ot", [P, 2, P])
    o = m.sb(tag + "o", [P, 2, HD])
    fold = m.sb(tag + "fold", [P, P])
    sc = [m.ps(tag + f"sc{b}") for b in range(G)]
    tp = [m.ps(tag + f"tp{i}") for i in range(2)]
    acc = m.ps(tag + "acc")
    fold_ld, v_done = m.sem(tag + "fold_ld"), m.sem(tag + "v")
    q_ld, s_done, mx_done, bias_done = m.sem(tag + "q_ld", 2), m.sem(tag + "s"), m.sem(tag + "mx"), m.sem(tag + "bias")
    e_done, t_done, hi_done, lo_done = m.sem(tag + "e"), m.sem(tag + "t"), m.sem(tag + "hi"), m.sem(tag + "lo")
    pv_done, ot_done, fold_done = m.sem(tag + "pv"), m.sem(tag + "ot"), m.sem(tag + "fold")
    tot_done, rden_done = m.sem(tag + "tot"), m.sem(tag + "rden")
    o_done, stored = m.sem(tag + "o"), m.sem(tag + "stored", 2)
    T_LAG, H_LAG, L_LAG = (0, 1, 1) if G > 2 else (0, 0, 0)
    if G > 2:
        OWN, BEFORE = {(1, 3): [0, 1], (1, G): [2, 3, 4, 5]}, {(0, 0): [6, 7], (0, G): list(range(8, 2 * G))}
        OUT_AT, FOLD_AT, NORM_AT = (1, 0), (1, 1), (1, 2)
    else:
        OWN, BEFORE = {(1, G): list(range(2 * G))}, {}
        OUT_AT = FOLD_AT = NORM_AT = (0, 0)

    def lagging(fn, lag, slot):
        for b in range(G):
            if min(b + lag, G) == slot:
                fn(b)

    def over_heads(eng, before, body, after):
        with eng.Fori(0, NKV) as g:
            eng.wait_ge(o_done, g * M)
            before(g)
            for p in range(2):
                body(g, p, p, 0)
            if V > 2:
                with eng.Fori(1, V - 1) as v:
                    for p in range(2):
                        body(g, 2 * v + p, p, v)
            for p in range(2):
                body(g, M - 2 + p, p, V - 1)
            after(g)

    none = lambda g: None
    fixed = lambda i: isinstance(i, int)
    is_last = lambda i: fixed(i) and i == M - 1
    in_first = lambda i: fixed(i) and i < 2
    with nc.Block() as block:

        @block.sync
        def _(sp):
            sp.dma_start(fold[:], a["fold"]).then_inc(fold_ld, 16)

            def load(g, i, p):
                sp.dma_start(q[:, p, :].bitcast(F32), s["q"][QPK * g + i // nq, i % nq + q0]).then_inc(q_ld[p], 16)

            def store(g, i, p):
                sp.wait_ge(o_done, g * M + i + 1)
                sp.dma_start(s["attn"][bass.ds((i % nq + q0) * P, P), bass.ds((QPK * g + i // nq) * HD, HD)], o[:, p, :]).then_inc(stored[p], 16)

            def before(g):
                for p in range(2):
                    load(g, p, p)

            def body(g, i, p, v):
                if not (fixed(i) and i >= M - 2):
                    sp.wait_ge(s_done, (g * M + i + 1) * G)
                    load(g, i + 2, p)
                if p == 1 and not in_first(i):
                    for k in range(2):
                        store(g, i - 3 + k, k)

            def after(g):
                for k in range(2):
                    store(g, M - 2 + k, k)

            over_heads(sp, before, body, after)
            for p in range(2):
                sp.wait_ge(stored[p], 16 * V * NKV)

        @block.scalar
        def _(act):
            def hi(g, i, p, v, b):
                t0, w = groups[b]
                act.wait_ge(t_done, (g * M + i) * G + b + 1)
                wait(act, pv_done, (g * V + v - 1) * 2 * G, 2 * b + 2 if not in_first(i) else 0)
                nc.scalar.activation(e_hi[:, t0:t0 + w, p, :], tp[(p * G + b) % 2][:, 0:w * P].rearrange("p (t n) -> p t n", n=P), ACT.Copy).then_inc(hi_done, 1)

            def out(g, v):
                act.wait_ge(pv_done, (g * V + v + 1) * 2 * G)
                nc.scalar.activation(ot[:], acc[:, 0:2 * P].rearrange("p (t n) -> p t n", n=P), ACT.Copy).then_inc(ot_done, 1)

            def body(g, i, p, v):
                act.wait_ge(bias_done, g * M + i + 1)
                for b in range(G + 1):
                    if b < G:
                        t0, w = groups[b]
                        wait(act, t_done, (g * M + i - 2) * G, b + 1 if not in_first(i) else 0)
                        if b == 0 and not in_first(i):
                            act.wait_ge(tot_done, g * M + i - 1)
                        nc.scalar.activation(e[:, p, t0 * P:(t0 + w) * P], sc[b][:, 0:w * P], ACT.Exp, bias=nbias[:, p:p + 1],
                                             accum_out=esum[:, p, b:b + 1]).then_inc(e_done, 1)
                    lagging(lambda k: hi(g, i, p, v, k), H_LAG, b)
                    if (p, b) == OUT_AT and not in_first(i):
                        out(g, v - 1)

            over_heads(act, none, body, lambda g: out(g, V - 1))

        @block.vector
        def _(dve):
            dve.wait_ge(fold_ld, 16)

            def maximum(g, i, b):
                dve.wait_ge(s_done, (g * M + i) * G + b + 1)
                nc.vector.reduce_max(mx[:, b:b + 1], sc[b][:, 0:groups[b][1] * P], AX.X).then_inc(mx_done, 1)

            def bias(g, i, p):
                dve.wait_ge(mx_done, (g * M + i + 1) * G)
                nc.vector.tensor_reduce(nbias[:, p:p + 1], mx[:], AX.X, ALU.max, negate=True).then_inc(bias_done, 1)

            def lo(g, i, p, b):
                t0, w = groups[b]
                dve.wait_ge(hi_done, (g * M + i) * G + b + 1)
                nc.vector.tensor_tensor(e_lo[:, t0:t0 + w, p, :], tp[(p * G + b) % 2][:, 0:w * P].rearrange("p (t n) -> p t n", n=P), e_hi[:, t0:t0 + w, p, :].bitcast(F32), ALU.subtract).then_inc(lo_done, 1)

            def total(g, i, p):
                dve.wait_ge(e_done, (g * M + i + 1) * G)
                if p == 0 and not in_first(i):
                    dve.wait_ge(rden_done, g * V + i // 2)
                nc.vector.reduce_sum(tot[:, p:p + 1], esum[:, p, :], AX.X).then_inc(tot_done, 1)

            def reciprocals(g, v):
                dve.wait_ge(tot_done, g * M + 2 * v + 2)
                nc.vector.reciprocal(rden[:], tot[:]).then_inc(rden_done, 1)

            def norm(g, v):
                dve.wait_ge(fold_done, g * V + v + 1)
                dve.wait_ge(rden_done, g * V + v + 1)
                for p in range(2):
                    dve.wait_ge(stored[p], 16 * (g * V + v))
                    nc.vector.tensor_scalar(o[:, p, :], acc[:, (2 + p) * P:(2 + p) * P + HD], rden[:, p:p + 1], None, ALU.mult).then_inc(o_done, 1)

            def before(g):
                nc.vector.tensor_copy(vcur[:], vres[:, 0:nk, g, :].bitcast(F32)).then_inc(v_done, 1)
                for b in range(G):
                    maximum(g, 0, b)
                bias(g, 0, 0)

            def body(g, i, p, v):
                for b in range(G + 1):
                    if b < G and not is_last(i):
                        maximum(g, i + 1, b)
                        if b == G - 1:
                            bias(g, i + 1, 1 - p)
                    lagging(lambda k: lo(g, i, p, k), L_LAG, b)
                    if (p, b) == NORM_AT and not in_first(i):
                        norm(g, v - 1)
                total(g, i, p)
                if p == 1:
                    reciprocals(g, v)

            over_heads(dve, before, body, lambda g: norm(g, V - 1))

        @block.tensor
        def _(pe):
            pe.wait_ge(fold_ld, 16)

            def scores(g, i, p, v, b):
                t0, w = groups[b]
                if b == 0:
                    pe.wait_ge(q_ld[p], 16 * (g * V + v + 1))
                wait(pe, e_done, (g * M + i - 1) * G, b + 1 if not (fixed(i) and i == 0) else 0)
                for k in range(2):
                    mm = nc.tensor.matmul(sc[b][:, 0:w * P], q[:, p, :], kres[:, g + NKV * k, t0 * P:(t0 + w) * P], start=(k == 0), stop=(k == 1))
                mm.then_inc(s_done, 1)

            def turned(g, i, p, b):
                t0, w = groups[b]
                pe.wait_ge(e_done, (g * M + i) * G + b + 1)
                wait(pe, lo_done, (g * M + i) * G - 2, b + 1 if not (fixed(i) and i * G + b < 2) else 0)
                for t in range(w):
                    mm = nc.tensor.transpose(tp[(p * G + b) % 2][:, t * P:(t + 1) * P], e[:, p, (t0 + t) * P:(t0 + t + 1) * P], keep["ident"][:])
                mm.then_inc(t_done, 1)

            def values(g, v, k):
                b = k // 2
                t0, w = groups[b]
                pe.wait_ge(lo_done, (g * M + 2 * v + 1) * G + b + 1)
                if k == 0:
                    pe.wait_ge(v_done, g + 1)
                    pe.wait_ge(o_done, g * M + 2 * v)
                for t in range(t0 + (k % 2) * (w // 2), t0 + (w if k % 2 else w // 2)):
                    nc.tensor.matmul(acc[:, 0:2 * P], vcur[:, t, :], e_hi[:, t].rearrange("p a n -> p (a n)"), start=(t == 0), stop=False)
                    mm = nc.tensor.matmul(acc[:, 0:2 * P], vcur[:, t, :], e_lo[:, t].rearrange("p a n -> p (a n)"), start=False, stop=(t == nk - 1))
                mm.then_inc(pv_done, 1)

            def folded(g, v):
                pe.wait_ge(ot_done, g * V + v + 1)
                for p in range(2):
                    mm = nc.tensor.matmul(acc[:, (2 + p) * P:(3 + p) * P], ot[:, p, :], fold[:], start=True, stop=True)
                mm.then_inc(fold_done, 1)

            def before(g):
                for b in range(G):
                    scores(g, 0, 0, 0, b)

            def body(g, i, p, v):
                for b in range(G + 1):
                    if b < G and not is_last(i):
                        scores(g, i + 1, 1 - p, v + p, b)
                    lagging(lambda k: turned(g, i, p, k), T_LAG, b)
                    for k in OWN.get((p, b), ()):
                        values(g, v, k)
                    if not in_first(i):
                        for k in BEFORE.get((p, b), ()):
                            values(g, v - 1, k)
                        if (p, b) == FOLD_AT:
                            folded(g, v - 1)

            def after(g):
                for b in (k for ks in BEFORE.values() for k in ks):
                    values(g, V - 1, b)
                folded(g, V - 1)

            over_heads(pe, before, body, after)


class OutWeights:

    def __init__(self, nc, m, layer, w):
        tag = f"ow{layer}_"
        self.nc, self.w, self.tag = nc, w, tag
        self.whi, self.wlo = m.sb(tag + "whi", [P, KD, D], F32R), m.sb(tag + "wlo", [P, KD, D], F32R)
        self.wst = m.sb(tag + "wst", [P, D])

    def signals(self, m):
        self.ld, self.hi, self.lo = (m.sem(self.tag + x) for x in ("ld", "hi", "lo"))

    def load(self, eng, k):
        eng.wait_ge(self.lo, k)
        eng.dma_start(self.wst[:], self.w[bass.ds(k * P, P), :]).then_inc(self.ld, 16)

    def high_part(self, act, k):
        act.wait_ge(self.ld, k * 16 + 16)
        self.nc.scalar.activation(self.whi[:, k, :], self.wst[:], ACT.Copy).then_inc(self.hi, 1)

    def low_part(self, pool, k):
        pool.wait_ge(self.hi, k + 1)
        self.nc.gpsimd.tensor_tensor(self.wlo[:, k, :], self.wst[:], self.whi[:, k, :].bitcast(F32), ALU.subtract).then_inc(self.lo, 1)


def fourier(nc, m, a, s, keep, out_weights):
    jobs = ((0, CT, "dft_ctx"), (CT, LT, "dft_lat"))
    H = LT // 2
    u = m.sb("fo_u", [P, NT, FW])
    ev, od = m.sb("fo_ev", [P, H - 1, FW]), m.sb("fo_od", [P, H - 1, FW])
    z = m.sb("fo_z", [P, H + 1 + 2, 3, FW])
    tabs = [m.sb("fo_" + name, [P, 2, R, P]) for _, R, name in jobs]
    head_tab, mix = m.sb("fo_head", [P, 2, P]), m.sb("fo_mix", [P, 2, P])
    g12 = m.sb("fo_g", [P, 2, 2, P])
    yt = m.sb("fo_yt", [P, 2, 4, P])
    o = m.sb("fo_o", [P, 2, FW])
    pg, py, po = m.ps("fo_pg"), [m.ps(f"fo_py{i}") for i in range(2)], [m.ps(f"fo_po{i}") for i in range(2)]
    ld, chain, z_done = m.sem("fo_ld"), m.sem("fo_chain"), m.sem("fo_z_done")
    g_mm, g_done = m.sem("fo_g_mm"), m.sem("fo_g_done")
    y_mm, y_out, o_mm, o_out, stored = m.sem("fo_y_mm"), m.sem("fo_y_out"), m.sem("fo_o_mm"), m.sem("fo_o_out"), m.sem("fo_stored", 2)
    out_weights.signals(m)
    outs = [(j, R, r, (H + 1 + r if j == 0 else min(r, R - r)), j == 1 and r > H) for j, (_, R, _) in enumerate(jobs) for r in range(R)]
    with nc.Block() as block:

        @block.sync
        def _(sp):
            sp.dma_start(head_tab[:], a["dft_head"].rearrange("c p n -> p c n")).then_inc(ld, 16)
            sp.dma_start(mix[:], a["fmix"].rearrange("c p n -> p c n")).then_inc(ld, 16)
            sp.dma_start(u[:], s["un"].rearrange("(t p) n -> p t n", p=P)).then_inc(ld, 16)
            for tab, (_, _, name) in zip(tabs, jobs):
                sp.dma_start(tab[:], a[name]).then_inc(ld, 16)
            for k in range(KD):
                out_weights.load(sp, k)
            for n, (j, R, r, _, _) in enumerate(outs):
                sp.wait_ge(o_out, n + 1)
                rows = s["four"][0:CTX] if j == 0 else s["four"][CTX:T]
                sp.dma_start(rows.rearrange("(m r) c -> r m c", r=R)[r], o[:, n % 2, :]).then_inc(stored[n % 2], 16)
            for i in range(2):
                sp.wait_ge(stored[i], 16 * (len(outs) // 2))

        @block.gpsimd
        def _(pool):
            for k in range(KD):
                out_weights.low_part(pool, k)

        @block.vector
        def _(dve):
            dve.wait_ge(ld, 80)
            c = Steps(dve, chain)
            c.did(nc.vector.tensor_tensor(z[:, H + 1, 0, :], u[:, 0], u[:, 1], ALU.add))
            c.did(nc.vector.tensor_tensor(z[:, H + 2, 0, :], u[:, 0], u[:, 1], ALU.subtract))
            x = u[:, CT:]
            c.did(nc.vector.tensor_tensor(ev[:], x[:, 1:H], x[:, LT - 1:H:-1], ALU.add))
            c.did(nc.vector.tensor_tensor(od[:], x[:, 1:H], x[:, LT - 1:H:-1], ALU.subtract))
            for r in range(H + 1):
                c.did(nc.vector.tensor_tensor(z[:, r, 0, :], x[:, 0], x[:, H], ALU.add if r % 2 == 0 else ALU.subtract))
            c.did(nc.vector.memset(z[:, 0:H + 1:H, 1:3, :], 0.0))
            for i in range(1, H):
                c.wait()
                for r in range(H + 1):
                    co = float(np.cos(2 * np.pi * ((i * r) % LT) / LT))
                    c.did(nc.vector.scalar_tensor_tensor(z[:, r, 0, :], ev[:, i - 1], co, z[:, r, 0, :], ALU.mult, ALU.add))
                for r in range(1, H):
                    si = -float(np.sin(2 * np.pi * ((i * r) % LT) / LT))
                    if i == 1:
                        c.did(nc.vector.tensor_scalar(z[:, r, 1, :], od[:, 0], si, None, ALU.mult))
                    else:
                        c.did(nc.vector.scalar_tensor_tensor(z[:, r, 1, :], od[:, i - 1], si, z[:, r, 1, :], ALU.mult, ALU.add))
            c.wait()
            nc.vector.tensor_scalar(z[:, 1:H, 2, :], z[:, 1:H, 1, :], -1.0, None, ALU.mult).then_inc(z_done, 1)
            for n in range(len(outs)):
                dve.wait_ge(o_mm, n + 1)
                if n >= 2:
                    dve.wait_ge(stored[n % 2], 16 * (n // 2))
                nc.vector.tensor_copy(o[:, n % 2, :], po[n % 2][:, 0:FW]).then_inc(o_out, 1)

        @block.scalar
        def _(act):
            for k in range(KD):
                out_weights.high_part(act, k)
            act.wait_ge(g_mm, 1)
            nc.scalar.activation(g12[:], pg[:].rearrange("p (c h n) -> p c h n", c=2, h=2), ACT.Copy).then_inc(g_done, 1)
            for n in range(len(outs)):
                act.wait_ge(y_mm, n + 1)
                if n >= 2:
                    act.wait_ge(o_mm, n - 1)
                nc.scalar.activation(yt[:, n % 2], py[n % 2][:].rearrange("p (c n) -> p c n", c=4), ACT.Copy).then_inc(y_out, 1)

        @block.tensor
        def _(pe):
            pe.wait_ge(ld, 80)
            for c in range(2):
                for h in range(2):
                    mm = nc.tensor.matmul(pg[:, (2 * c + h) * P:(2 * c + h + 1) * P], head_tab[:, c, :], mix[:, h, :], start=True, stop=True)
            mm.then_inc(g_mm, 1)
            pe.wait_ge(z_done, 1)

            def mixed(n):
                pe.wait_ge(y_out, n + 1)
                if n == 0:
                    pe.wait_ge(g_done, 1)
                if n >= 2:
                    pe.wait_ge(o_out, n - 1)
                for h in range(2):
                    for c in range(2):
                        mm = nc.tensor.matmul(po[n % 2][:, h * P:(h + 1) * P], yt[:, n % 2, 2 * h + c, :], g12[:, c, h, :], start=(c == 0), stop=(c == 1))
                mm.then_inc(o_mm, 1)

            for n, (j, R, r, slot, conj) in enumerate(outs):
                if n >= 2:
                    pe.wait_ge(y_out, n - 1)
                co, si = tabs[j][:, 0, r, :], tabs[j][:, 1, r, :]
                re, im, nim = (z[:, slot, i, :] for i in range(3))
                if conj:
                    im, nim = nim, im
                for h in range(2):
                    cols = slice(h * P, (h + 1) * P)
                    for c, terms in enumerate((((re, co), (im, si)), ((re, si), (nim, co)))):
                        if j == 0:
                            terms = terms[:1]
                        dst = py[n % 2][:, (2 * h + c) * P:(2 * h + c + 1) * P]
                        for i, (lhs, rhs) in enumerate(terms):
                            mm = nc.tensor.matmul(dst, lhs[:, cols], rhs, start=(i == 0), stop=(i == len(terms) - 1))
                mm.then_inc(y_mm, 1)
                if n:
                    mixed(n - 1)
            mixed(len(outs) - 1)


def mixer_out(nc, m, a, s, keep, layer, out, out_weights):
    L0 = layer == 0
    tag = f"mo{layer}_"
    t0 = 0 if L0 else CT
    N = NT - t0
    whi, wlo = out_weights.whi, out_weights.wlo
    x_src = a["x"] if L0 else s["x1"]
    NIN = 2 if L0 else 4
    ins = m.sb(tag + "in", [P, 2, NIN, D])
    x = m.sb(tag + "x", [P, 2, D])
    sg = m.sb(tag + "sg", [P, NIN // 2, D])
    y = m.sb(tag + "y", [P, 2, D])
    y_hi, y_lo = m.sb(tag + "y_hi", [P, 2, KD, P], F32R), m.sb(tag + "y_lo", [P, 2, KD, P], F32R)
    gate = m.sb(tag + "gate", [P, 2 if L0 else 1, D])
    gain, beta = m.sb(tag + "gain", [P, D]), m.sb(tag + "beta", [P, D])
    r = m.sb(tag + "r", [P, D])
    fin = m.sb(tag + "fin", [P, 2, D])
    eps, held = m.sb(tag + "eps", [P, 1]), m.sb(tag + "held", [P, 1])
    stats, mv, rstd, half = m.sb(tag + "stats", [P, 2, 6]), m.sb(tag + "mv", [P, 2]), m.sb(tag + "rstd", [P, 1]), m.sb(tag + "half", [P, 1])
    tp, acc = [m.ps(tag + f"tp{i}", (P, 2, 512)) for i in range(2)], [m.ps(tag + f"acc{i}", (P, 2, 512)) for i in range(2)]
    const = m.sem(tag + "const")
    in_ld, x_ld, y_done, x_used = m.sem(tag + "in_ld", 2), m.sem(tag + "x_ld", 2), m.sem(tag + "y_done", 2), m.sem(tag + "x_used", 2)
    sg_done, tr_done, hi_done, lo_done = m.sem(tag + "sg_done"), m.sem(tag + "tr"), m.sem(tag + "hi"), m.sem(tag + "lo")
    mm_done, chain, var_done, rstd_done = m.sem(tag + "mm"), m.sem(tag + "chain"), m.sem(tag + "var"), m.sem(tag + "rstd_d")
    nrm_done, fin_done, stored, ready, h_sum, zz = m.sem(tag + "nrm"), m.sem(tag + "fin"), m.sem(tag + "stored", 2), m.sem(tag + "ready"), m.sem(tag + "hsum"), m.sem(tag + "zz")
    half_done = m.sem(tag + "half_done")
    acc_out = m.sem(tag + "acc_out")

    first = lambda n: isinstance(n, int) and n == 0
    with nc.Block() as block:

        @block.sync
        def _(sp):
            sp.dma_start(gain[:], a["post_gain"][layer:layer + 1].broadcast_to([P, D])).then_inc(const, 16)
            sp.dma_start(beta[:], a["post_bias"][layer:layer + 1].broadcast_to([P, D])).then_inc(const, 16)
            for i in range(2 if L0 else 1):
                sp.dma_start(gate[:, i, :], s["gates"][2 * layer + i]).then_inc(const, 16)

            def inputs(n, p, v):
                sp.wait_ge(y_done[p], v)
                rows = bass.ds((n + t0) * P, P)
                if L0:
                    sp.dma_start(ins[:, p, 0, 0:QW], s["attn"][rows, :]).then_inc(in_ld[p], 16)
                    sp.dma_start(ins[:, p, 0, QW:D], s["four"][rows, :]).then_inc(in_ld[p], 16)
                    sp.dma_start(ins[:, p, 1, :], s["proj0"][rows, C_GATE:W0_COLS]).then_inc(in_ld[p], 16)
                else:
                    for d in range(2):
                        sp.dma_start(ins[:, p, d, :], s["h"][d, bass.ds(n * P, P), :]).then_inc(in_ld[p], 16)
                    sp.dma_start(ins[:, p, 2:4, :], s["proj1"][rows, C1_O:W1_COLS].rearrange("p (i n) -> p i n", i=2)).then_inc(in_ld[p], 16)

            def residual(n, p, v):
                sp.wait_ge(x_used[p], v)
                sp.dma_start(x[:, p, :], x_src[bass.ds((n + t0) * P, P), :]).then_inc(x_ld[p], 16)

            def before():
                inputs(0, 0, 0)
                inputs(1, 1, 0)

            def body(n, p, v):
                tile(inputs, N, n, p, v, 2)
                residual(n, p, v)

            over_turns(sp, N, before, body)

        @block.scalar
        def _(act):
            act.wait_ge(const, 16 * (4 if L0 else 3))
            fn = ACT.Silu if L0 else ACT.Sigmoid

            def gates(n, p, v):
                act.wait_ge(in_ld[p], 48 * v + 48)
                if not first(n):
                    act.wait_ge(y_done[1 - p], v + p)
                nc.scalar.activation(sg[:], ins[:, p, NIN // 2:NIN, :], fn).then_inc(sg_done, 1)

            def high_part(n, p, v):
                act.wait_ge(tr_done, n + 1)
                if not (isinstance(n, int) and n < 2):
                    act.wait_ge(mm_done, n - 1)
                nc.scalar.activation(y_hi[:, p], tp[p][:].rearrange("p a (k n) -> p (a k) n", n=P), ACT.Copy).then_inc(hi_done, 1)

            def before():
                gates(0, 0, 0)
                gates(1, 1, 0)
                high_part(0, 0, 0)

            def body(n, p, v):
                tile(gates, N, n, p, v, 2)
                tile(high_part, N, n, p, v, 1)

            over_turns(act, N, before, body)

        @block.gpsimd
        def _(pool):
            nc.gpsimd.memset(half[:], -0.5).then_inc(ready, 1)
            nc.gpsimd.memset(eps[:], EPS).then_inc(ready, 1)
            pool.wait_ge(ready, 2)
            pool.wait_ge(const, 16 * (4 if L0 else 3))

            def post(n, p, v):
                pool.wait_ge(var_done, n + 1)
                nc.gpsimd.tensor_tensor(rstd[:], mv[:, 1:2], eps[:], ALU.add).then_inc(ready, 1)
                pool.wait_ge(ready, n + 3)
                nc.gpsimd.tensor_tensor(rstd[:], rstd[:], half[:], ALU.pow).then_inc(rstd_done, 1)
                pool.wait_ge(nrm_done, n + 1)
                nc.gpsimd.tensor_tensor(fin[:, p, :], fin[:, p, :], beta[:], ALU.add).then_inc(fin_done, 1)
                pool.wait_ge(fin_done, n + 1)
                rows = out[bass.ds(n * P, P), :]
                pool.dma_start(rows, fin[:, p, :]).then_inc(stored[p], 16)

            def gated(n, p, v):
                if not L0:
                    pool.wait_ge(in_ld[p], 48 * v + 48)
                    nc.gpsimd.tensor_tensor(ins[:, p, 0, :], ins[:, p, 0, :], ins[:, p, 1, :], ALU.add).then_inc(h_sum, 1)
                    pool.wait_ge(sg_done, n + 1)
                    nc.gpsimd.tensor_tensor(ins[:, p, 3, :], ins[:, p, 3, :], sg[:, 1, :], ALU.mult).then_inc(zz, 1)

            def before():
                gated(0, 0, 0)
                gated(1, 1, 0)

            def body(n, p, v):
                tile(gated, N, n, p, v, 2)
                tile(post, N, n, p, v, -1)

            over_turns(pool, N, before, body, lambda: post(N - 1, 1, N // 2 - 1))
            for p in range(2):
                pool.wait_ge(stored[p], 16 * (N // 2))

        @block.vector
        def _(dve):
            dve.wait_ge(const, 16 * (4 if L0 else 3))
            K = 3

            def post(n, p, v):
                kind = (n * -1 + (NT + CT - 1)) // NT if L0 else 0
                c = Steps(dve, chain, n * K)
                dve.wait_ge(mm_done, n + 1)
                dve.wait_ge(nrm_done, n)
                nc.vector.tensor_tensor(r[:], acc[p][:].rearrange("p a n -> p (a n)"), gate[:, kind, :], ALU.mult).then_inc(acc_out, 1)
                dve.wait_ge(acc_out, n + 1)
                dve.wait_ge(x_ld[p], 16 * v + 16)
                nc.vector.scalar_tensor_tensor(r[:], x[:, p, :], ALPHA, r[:], ALU.mult, ALU.add).then_inc(x_used[p], 1)
                dve.wait_ge(x_used[p], v + 1)
                for h in range(2):
                    c.did(nc.vector.bn_stats(stats[:, h, :], r[:, h * 512:(h + 1) * 512]))
                c.wait()
                nc.vector.memset(held[:], 0.0)
                nc.vector.bn_aggr(mv[:], stats[:].rearrange("p a b -> p (a b)")).then_inc(var_done, 1)
                dve.wait_ge(rstd_done, n + 1)
                c.did(nc.vector.tensor_scalar(r[:], r[:], mv[:, 0:1], rstd[:], ALU.subtract, ALU.mult))
                c.wait()
                dve.wait_ge(stored[p], 16 * v)
                nc.vector.tensor_tensor(fin[:, p, :], r[:], gain[:], ALU.mult).then_inc(nrm_done, 1)
                assert c.n == K

            def gated(n, p, v):
                dve.wait_ge(in_ld[p], 48 * v + 48)
                dve.wait_ge(sg_done, n + 1)
                if not (isinstance(n, int) and n < 2):
                    dve.wait_ge(tr_done, n - 1)
                if L0:
                    nc.vector.tensor_tensor(y[:, p, :], ins[:, p, 0, :], sg[:, 0, :], ALU.mult).then_inc(y_done[p], 1)
                else:
                    dve.wait_ge(h_sum, n + 1)
                    nc.vector.tensor_tensor(y[:, p, :], ins[:, p, 0, :], sg[:, 0, :], ALU.mult).then_inc(half_done, 1)
                    dve.wait_ge(half_done, n + 1)
                    dve.wait_ge(zz, n + 1)
                    nc.vector.tensor_tensor(y[:, p, :], y[:, p, :], ins[:, p, 3, :], ALU.mult).then_inc(y_done[p], 1)

            def low_part(n, p, v):
                dve.wait_ge(hi_done, n + 1)
                nc.vector.tensor_tensor(y_lo[:, p], tp[p][:].rearrange("p a (k n) -> p (a k) n", n=P), y_hi[:, p].bitcast(F32), ALU.subtract).then_inc(lo_done, 1)

            def before():
                gated(0, 0, 0)
                gated(1, 1, 0)
                low_part(0, 0, 0)

            def body(n, p, v):
                tile(gated, N, n, p, v, 2)
                tile(low_part, N, n, p, v, 1)
                tile(post, N, n, p, v, -1)

            over_turns(dve, N, before, body, lambda: post(N - 1, 1, N // 2 - 1))

        @block.tensor
        def _(pe):
            def products(n, p):
                pe.wait_ge(lo_done, n + 1)
                if not (isinstance(n, int) and n < 2):
                    pe.wait_ge(acc_out, n - 1)
                for h in range(2):
                    for k in range(KD):
                        mm = split_mm(nc, acc[p][:, h, :], y_hi[:, p, k, :], y_lo[:, p, k, :], whi[:, k, h * CH:(h + 1) * CH], wlo[:, k, h * CH:(h + 1) * CH], k == 0, k == KD - 1)
                mm.then_inc(mm_done, 1)

            def turned(n, p, v):
                pe.wait_ge(y_done[p], v + 1)
                if not (isinstance(n, int) and n < 2):
                    pe.wait_ge(lo_done, n - 1)
                for k in range(KD):
                    tr = nc.tensor.transpose(tp[p][:, k // 4, (k % 4) * P:(k % 4 + 1) * P], y[:, p, k * P:(k + 1) * P], keep["ident"][:])
                tr.then_inc(tr_done, 1)

            def body(n, p, v):
                tile(turned, N, n, p, v, 1)
                products(n, p)

            over_turns(pe, N, lambda: turned(0, 0, 0), body)
    m.end()


def gate_rows(nc, m, a, keep, graw, mrow, cols, dec):
    R = NR
    full = lambda n: m.sb("gr_" + n, [R, T])
    lf, rst, neg, cum, cmax, tmp = (full(n) for n in ("lf", "rst", "neg", "cum", "cmax", "tmp"))
    arrs = [m.sb("gr_arr0", [P, T]), m.sb("gr_arr1", [P, T])]
    small = lambda n: m.sb("gr_" + n, [R, NT])
    tot, amax, tot_t, amax_t, m_t, m_in_t, m_in, m_last = (small(n) for n in ("tot", "amax", "tot_t", "amax_t", "m_t", "m_in_t", "m_in", "m_last"))
    decr = m.sb("gr_decr", [P, NT])
    sel = m.sb("gr_sel", [P, 2 * MH, P])
    tp = [m.ps(f"gr_tp{i}") for i in range(2)]
    pd = m.ps("gr_pd")
    ld, ready, v_done, s_done = m.sem("gr_ld"), m.sem("gr_ready"), m.sem("gr_v"), m.sem("gr_s")
    diff_done, scaled = m.sem("gr_diff"), m.sem("gr_scaled")
    tr_done, tr_out, d_mm = m.sem("gr_tr"), m.sem("gr_tr_out"), m.sem("gr_d_mm")
    FW_, BW_ = slice(0, 32), slice(32, R)
    blocks = [(i, t0, min(4, NT - t0)) for i in range(2) for t0 in range(0, NT, 4)]
    ch = lambda ap: ap.rearrange("p (c n) -> p c n", n=P)
    bc = lambda ap: ap.unsqueeze(2).broadcast_to([R, NT, P])
    with nc.Block() as block:

        @block.sync
        def _(sp):
            sp.dma_start(sel[:], a["sel"]).then_inc(ld, 16)

        @block.gpsimd
        def _(pool):
            for t in (arrs[0], arrs[1], mrow, decr):
                nc.gpsimd.memset(t[:], 0.0).then_inc(ready, 1)

        @block.scalar
        def _(act):
            nc.scalar.activation(tmp[:], graw[64:64 + R, :], ACT.Abs).then_inc(s_done, 1)
            act.wait_ge(s_done, 1)
            nc.scalar.activation(tmp[:], tmp[:], ACT.Exp, scale=-1.0).then_inc(s_done, 1)
            act.wait_ge(s_done, 2)
            nc.scalar.activation(tmp[:], tmp[:], ACT.Ln, bias=1.0).then_inc(s_done, 1)
            for n, (dst, sc) in enumerate(((arrs[0][64:64 + R, :], 1.0), (arrs[1][0:R, :], 1.0), (arrs[1][64:64 + R, :], -1.0), (decr[0:R, :], 1.0))):
                act.wait_ge(diff_done, n + 1)
                nc.scalar.activation(dst, dst, ACT.Exp, scale=sc).then_inc(s_done, 1)

        @block.vector
        def _(dve):
            c = Steps(dve, v_done)

            def do(ins):
                c.did(ins)
                c.wait()

            V = nc.vector
            do(V.memset(rst[:], 1.0))
            do(V.memset(rst[FW_, 0::P], 0.0))
            do(V.memset(rst[BW_, P - 1::P], 0.0))
            do(V.tensor_scalar(neg[:], rst[:], -1.0, MASKED, ALU.add, ALU.mult))
            do(V.tensor_scalar(lf[:], graw[64:64 + R, :], 0.0, None, ALU.min))
            dve.wait_ge(s_done, 3)
            do(V.tensor_tensor(lf[:], lf[:], tmp[:], ALU.subtract))
            do(V.tensor_tensor_scan(cum[FW_, :], rst[FW_, :], lf[FW_, :], 0.0, ALU.mult, ALU.add))
            do(V.tensor_tensor_scan(cum[BW_, ::-1], rst[BW_, ::-1], lf[BW_, ::-1], 0.0, ALU.mult, ALU.add))
            dve.wait_ge(ready, 4)
            av = arrs[0][0:R, :]
            do(V.tensor_tensor(av, graw[0:R, :], cum[:], ALU.subtract))
            do(V.tensor_tensor_scan(cmax[FW_, :], neg[FW_, :], arrs[0][FW_, :], -MASKED, ALU.add, ALU.max))
            do(V.tensor_tensor_scan(cmax[BW_, ::-1], neg[BW_, ::-1], arrs[0][BW_, ::-1], -MASKED, ALU.add, ALU.max))
            for dst, src in ((tot, cum), (amax, cmax)):
                do(V.tensor_copy(dst[FW_, :], src[FW_, P - 1::P]))
                do(V.tensor_copy(dst[BW_, :], src[BW_, 0::P]))
            for dst, src in ((tot_t, tot), (amax_t, amax)):
                do(V.tensor_copy(dst[FW_, :], src[FW_, :]))
                do(V.tensor_copy(dst[BW_, 0:CT], src[BW_, CT - 1::-1]))
                do(V.tensor_copy(dst[BW_, CT:NT], src[BW_, NT - 1:CT - 1:-1]))
            do(V.tensor_tensor_scan(m_t[:], amax_t[:], tot_t[:], 0.0, ALU.max, ALU.add))
            do(V.memset(m_in_t[:, 0:1], 0.0))
            do(V.tensor_copy(m_in_t[:, 1:NT], m_t[:, 0:NT - 1]))
            do(V.tensor_copy(m_in[FW_, :], m_in_t[FW_, :]))
            do(V.tensor_copy(m_in[BW_, CT - 1::-1], m_in_t[BW_, 0:CT]))
            do(V.tensor_copy(m_in[BW_, NT - 1:CT - 1:-1], m_in_t[BW_, CT:NT]))
            do(V.tensor_tensor(m_last[:], m_in[:], amax[:], ALU.max))
            do(V.tensor_tensor(ch(mrow[0:R, :]), ch(cmax[:]), bc(m_in[:]), ALU.max))
            do(V.tensor_tensor(ch(cmax[:]), ch(av), bc(m_last[:]), ALU.subtract))
            V.tensor_copy(arrs[0][64:64 + R, :], cmax[:]).then_inc(diff_done, 1)
            V.tensor_tensor(ch(arrs[1][0:R, :]), bc(m_in[:]), ch(mrow[0:R, :]), ALU.subtract).then_inc(diff_done, 1)
            do(V.tensor_tensor(tmp[:], cum[:], mrow[0:R, :], ALU.add))
            V.tensor_copy(arrs[1][64:64 + R, :], tmp[:]).then_inc(diff_done, 1)
            V.tensor_tensor(decr[0:R, :], m_in[:], m_last[:], ALU.subtract).then_inc(diff_done, 1)
            dve.wait_ge(s_done, 4)
            V.tensor_scalar(arrs[0][64:64 + R, :], arrs[0][64:64 + R, :], float(MD) ** -0.5, None, ALU.mult).then_inc(scaled, 1)
            for n, (i, t0, w) in enumerate(blocks):
                dve.wait_ge(tr_done, n + 1)
                src = tp[n % 2][:, 0:w * P].rearrange("p (t g r) -> p t g r", g=4, r=32)
                for t in range(w):
                    V.tensor_copy(cols[:, t0 + t, i], src[:, t, :, 0:MH]).then_inc(tr_out, 1)
            dve.wait_ge(d_mm, 1)
            V.tensor_copy(dec[:], pd[:, 0:2 * MH * NT].rearrange("p (r c) -> p r c", c=NT)).then_inc(v_done, 1)

        @block.tensor
        def _(pe):
            out_n = 0
            for n, (i, t0, w) in enumerate(blocks):
                if n == 0:
                    pe.wait_ge(scaled, 1)
                if i == 1 and t0 == 0:
                    pe.wait_ge(s_done, 6)
                if n >= 2:
                    pe.wait_ge(tr_out, sum(b[2] for b in blocks[:n - 1]))
                for t in range(w):
                    tr = nc.tensor.transpose(tp[n % 2][:, t * P:(t + 1) * P], arrs[i][:, (t0 + t) * P:(t0 + t + 1) * P], keep["ident"][:])
                tr.then_inc(tr_done, 1)
            pe.wait_ge(s_done, 7)
            pe.wait_ge(ld, 16)
            for r in range(2 * MH):
                mm = nc.tensor.matmul(pd[:, r * NT:(r + 1) * NT], sel[:, r, :], decr[:], start=True, stop=True)
            mm.then_inc(d_mm, 1)


def mlstm(nc, m, a, s, keep, mrow, cols, dec, out_weights):
    VC = MD + 2
    kb = m.sb("ml_k", [P, 2, 2, D])
    vb = m.sb("ml_v", [P, 2, 2, MH, VC])
    qb = m.sb("ml_q", [P, 2, 2, D])
    qkt = m.sb("ml_qkt", [P, 2, 4, P])
    ccol = m.sb("ml_ccol", [P, 2, 2, 2, 4, MH])
    dcol = m.sb("ml_dcol", [P, 2, 2, 2 * MH])
    dw, sw = m.sb("ml_dw", [P, 2, P]), m.sb("ml_sw", [P, 2, P])
    vw = m.sb("ml_vw", [P, 2, VC])
    state = m.sb("ml_state", [P, 2, MH, 2, VC])
    inter, total = m.sb("ml_inter", [P, 2, VC]), m.sb("ml_total", [P, 2, VC])
    den = m.sb("ml_den", [P, 3])
    h = m.sb("ml_h", [P, 2, 2, D])
    sel, mask = m.sb("ml_sel", [P, 2 * MH, P]), m.sb("ml_mask", [P, 2, P])
    tp = [m.ps(f"ml_tp{i}") for i in range(2)]
    psc, pmx, pin, pst = m.ps("ml_psc"), m.ps("ml_pmx"), m.ps("ml_pin"), m.ps("ml_pst")
    pup = m.ps("ml_pup", (P, 2, 512))
    const, ready = m.sem("ml_const"), m.sem("ml_ready")
    ld = [[m.sem(f"ml_ld{d}{p}") for p in range(2)] for d in range(2)]
    col_done, tr_done, tr_out, sc_mm, mx_mm = (m.sem("ml_" + x) for x in ("col", "tr", "tr_out", "sc", "mx"))
    dw_done, sw_done, in_mm, st_mm, up_mm, vw_done = (m.sem("ml_" + x) for x in ("dw", "sw", "in", "st", "up", "vw"))
    inter_done, total_done, den_done, h_done, up_half, up_done = (m.sem("ml_" + x) for x in ("inter", "total", "den", "h", "up_half", "up_done"))
    stored = [[m.sem(f"ml_stored{d}{p}") for p in range(2)] for d in range(2)]
    U = [(p, d, hh) for p in range(2) for d in range(2) for hh in range(MH)]
    NU = len(U)
    TURNS = LT // 2
    assert TURNS == KD
    out_weights.signals(m)
    chunk = lambda v, p, d: CT + 2 * v + p if d == 0 else v * -2 + (NT - 1 - p)
    ctx_chunk = lambda p, d: p if d == 0 else CT - 1 - p
    with nc.Block() as block:

        @block.sync
        def _(sp):
            sp.dma_start(sel[:], a["sel"]).then_inc(const, 16)
            sp.dma_start(mask[:], a["mask"].rearrange("d p n -> p d n")).then_inc(const, 16)
            sp.wait_ge(ready, 2)

            def load(d, p, c, with_q):
                rows = bass.ds(c * P, P)
                sp.dma_start(kb[:, d, p, :], s["proj1"][rows, C1_K:C1_K + D]).then_inc(ld[d][p], 16)
                sp.dma_start(vb[:, d, p, :, 0:MD], s["proj1"][rows, C1_V:C1_V + D].rearrange("p (h n) -> p h n", n=MD)).then_inc(ld[d][p], 16)
                if with_q:
                    sp.dma_start(qb[:, d, p, :], s["proj1"][rows, C1_Q:C1_Q + D]).then_inc(ld[d][p], 16)

            for p in range(2):
                for d in range(2):
                    load(d, p, ctx_chunk(p, d), False)
            with sp.Fori(0, TURNS) as v:
                out_weights.load(sp, v)
                for p in range(2):
                    for d in range(2):
                        sp.wait_ge(up_done, NU * v + p * 2 * MH + (d + 1) * MH)
                        load(d, p, chunk(v, p, d), True)

        @block.gpsimd
        def _(pool):
            nc.gpsimd.memset(vb[:, :, :, :, MD:MD + 1], 1.0).then_inc(ready, 1)
            nc.gpsimd.memset(vb[:, :, :, :, MD + 1:VC], 0.0).then_inc(ready, 1)

            def weighted(u, base, ldv, cv):
                p, d, hh = U[u]
                pool.wait_ge(ld[d][p], ldv)
                pool.wait_ge(col_done, cv + 2 * (p * 2 + d) + 2)
                wait(pool, up_mm, base, u - 1)
                nc.gpsimd.tensor_tensor(vw[:, u % 2, :], vb[:, d, p, hh, :], ccol[:, p, d, 0, 2 + d, hh:hh + 1].broadcast_to([P, VC]), ALU.mult).then_inc(vw_done, 1)

            def store(v, p, d):
                pool.wait_ge(h_done, NU * v + (p * 2 + d + 1) * MH)
                pool.dma_start(s["h"][d, bass.ds((chunk(v, p, d) - CT) * P, P), :], h[:, d, p, :]).then_inc(stored[d][p], 16)

            for u in range(NU):
                weighted(u, 0, 32, 0)
            with pool.Fori(0, TURNS) as v:
                pool.wait_ge(up_mm, NU * v + NU)
                for u in range(NU):
                    weighted(u, NU * v + NU, 48 * v + 80, 8 * v + 8)
                    if u == MH:
                        out_weights.low_part(pool, v)
                    if u % MH == MH - 1 and u > MH:
                        store(v, *divmod(u // MH - 1, 2))
                store(v, 1, 1)
            for d in range(2):
                for p in range(2):
                    pool.wait_ge(stored[d][p], 16 * TURNS)

        @block.scalar
        def _(act):
            with act.Fori(0, TURNS) as v:
                b = NU * v

                def evacuate(u):
                    act.wait_ge(tr_done, b + u + 1)
                    act.wait_ge(st_mm, b + max(u - 1, 0))
                    nc.scalar.activation(qkt[:, u % 2], tp[u % 2][:].rearrange("p (k n) -> p k n", n=P), ACT.Copy).then_inc(tr_out, 1)

                def decays(u):
                    p, d, hh = U[u]
                    act.wait_ge(mx_mm, b + u + 1)
                    act.wait_ge(col_done, 8 * v + 8 + 2 * (p * 2 + d) + 2)
                    act.wait_ge(sw_done, b + max(u - 1, 0))
                    nc.scalar.activation(dw[:, u % 2, :], pmx[:, 0:P], ACT.Exp, bias=ccol[:, p, d, 0, d, hh:hh + 1], scale=-1.0).then_inc(dw_done, 1)

                def from_state(u):
                    p, d, hh = U[u]
                    act.wait_ge(st_mm, b + u + 1)
                    act.wait_ge(total_done, b + max(u - 1, 0))
                    nc.scalar.activation(inter[:, u % 2, :], pst[:, 0:VC], ACT.Copy, scale=ccol[:, p, d, 1, d, hh:hh + 1]).then_inc(inter_done, 1)

                evacuate(0)
                for u in range(NU):
                    if u + 1 < NU:
                        evacuate(u + 1)
                    if u == MH:
                        out_weights.high_part(act, v)
                    decays(u)
                    if u:
                        from_state(u - 1)
                from_state(NU - 1)

        @block.vector
        def _(dve):
            V = nc.vector
            V.memset(state[:], 0.0).then_inc(up_half, 1)

            def columns(p, d, c, seen):
                dve.wait_ge(up_done, seen)
                V.tensor_copy(ccol[:, p, d], cols[:, c]).then_inc(col_done, 1)
                V.tensor_copy(dcol[:, p, d, :], dec[:, :, c]).then_inc(col_done, 1)

            def update(u, base, cv):
                p, d, hh = U[u]
                dve.wait_ge(up_mm, base + u + 1)
                dve.wait_ge(col_done, cv + 2 * (p * 2 + d) + 2)
                dve.wait_ge(up_half, base + u + 1)
                for k, sem in enumerate((up_half, up_done)):
                    V.scalar_tensor_tensor(state[:, d, hh, k, :], state[:, d, hh, k, :], dcol[:, p, d, d * MH + hh:d * MH + hh + 1], pup[:, k, 0:VC], ALU.mult, ALU.add).then_inc(sem, 1)

            for p in range(2):
                for d in range(2):
                    columns(p, d, ctx_chunk(p, d), 0)
            for u in range(NU):
                update(u, 0, 0)
            with dve.Fori(0, TURNS) as v:
                b = NU * v
                for p in range(2):
                    for d in range(2):
                        columns(p, d, chunk(v, p, d), b + NU)

                def weights(u):
                    dve.wait_ge(sc_mm, b + u + 1)
                    dve.wait_ge(dw_done, b + u + 1)
                    dve.wait_ge(in_mm, b + max(u - 1, 0))
                    V.scalar_tensor_tensor(sw[:, u % 2, :], psc[:, 0:P], float(MD) ** -0.5, dw[:, u % 2, :], ALU.mult, ALU.mult).then_inc(sw_done, 1)

                def outputs(u):
                    p, d, hh = U[u]
                    dve.wait_ge(in_mm, b + u + 1)
                    dve.wait_ge(inter_done, b + u + 1)
                    dve.wait_ge(h_done, b + max(u - 1, 0))
                    V.tensor_tensor(total[:, u % 2, :], pin[:, 0:VC], inter[:, u % 2, :], ALU.add).then_inc(total_done, 1)
                    dve.wait_ge(total_done, b + u + 1)
                    c = Steps(dve, den_done, 3 * (b + u))
                    x = total[:, u % 2, MD:MD + 1]
                    c.did(V.scalar_tensor_tensor(den[:, 0:1], x, -1.0, x, ALU.mult, ALU.max))
                    c.wait()
                    c.did(V.tensor_tensor(den[:, 1:2], den[:, 0:1], ccol[:, p, d, 1, 2 + d, hh:hh + 1], ALU.max))
                    c.wait()
                    c.did(V.reciprocal(den[:, 2:3], den[:, 1:2]))
                    c.wait()
                    if hh == 0:
                        dve.wait_ge(stored[d][p], 16 * v)
                    V.tensor_scalar(h[:, d, p, hh * MD:(hh + 1) * MD], total[:, u % 2, 0:MD], den[:, 2:3], None, ALU.mult).then_inc(h_done, 1)

                for u in range(NU):
                    weights(u)
                    if u:
                        outputs(u - 1)
                        update(u - 1, b + NU, 8 * v + 8)
                outputs(NU - 1)
                update(NU - 1, b + NU, 8 * v + 8)

        @block.tensor
        def _(pe):
            mm = nc.tensor.matmul

            def update(u, base):
                p, d, hh = U[u]
                pe.wait_ge(vw_done, base + u + 1)
                pe.wait_ge(up_done, base + u)
                for k in range(2):
                    x = mm(pup[:, k, 0:VC], kb[:, d, p, hh * MD + k * P:hh * MD + (k + 1) * P], vw[:, u % 2, :], start=True, stop=True)
                x.then_inc(up_mm, 1)

            for u in range(NU):
                update(u, 0)
            pe.wait_ge(const, 32)
            with pe.Fori(0, TURNS) as v:
                b = NU * v

                def turned(u):
                    p, d, hh = U[u]
                    pe.wait_ge(ld[d][p], 48 * v + 80)
                    pe.wait_ge(tr_out, b + max(u - 1, 0))
                    for k, src in enumerate((qb, qb, kb, kb)):
                        x = nc.tensor.transpose(tp[u % 2][:, k * P:(k + 1) * P], src[:, d, p, hh * MD + (k % 2) * P:hh * MD + (k % 2 + 1) * P], keep["ident"][:])
                    x.then_inc(tr_done, 1)

                def scores(u):
                    p, d, hh = U[u]
                    pe.wait_ge(tr_out, b + u + 1)
                    pe.wait_ge(sw_done, b + u)
                    for k in range(2):
                        x = mm(psc[:, 0:P], qkt[:, u % 2, 2 + k, :], qkt[:, u % 2, k, :], start=(k == 0), stop=(k == 1))
                    x.then_inc(sc_mm, 1)
                    pe.wait_ge(dw_done, b + u)
                    mm(pmx[:, 0:P], sel[:, d * MH + hh, :], mrow[:, bass.ds(chunk(v, p, d) * P, P)], start=True, stop=False)
                    mm(pmx[:, 0:P], keep["ident"][:], mask[:, d, :], start=False, stop=True).then_inc(mx_mm, 1)

                def outputs(u):
                    p, d, hh = U[u]
                    pe.wait_ge(sw_done, b + u + 1)
                    pe.wait_ge(total_done, b + u)
                    mm(pin[:, 0:VC], sw[:, u % 2, :], vb[:, d, p, hh, :], start=True, stop=True).then_inc(in_mm, 1)
                    pe.wait_ge(inter_done, b + u)
                    pe.wait_ge(up_done, b + NU + max(u - 2 * MH + 1, 0) if u >= 2 * MH else b + u + 2 * MH + 1)
                    for k in range(2):
                        x = mm(pst[:, 0:VC], qkt[:, u % 2, k, :], state[:, d, hh, k, :], start=(k == 0), stop=(k == 1))
                    x.then_inc(st_mm, 1)

                turned(0)
                for u in range(NU):
                    if u + 1 < NU:
                        turned(u + 1)
                    scores(u)
                    if u:
                        outputs(u - 1)
                        update(u - 1, b + NU)
                outputs(NU - 1)
                update(NU - 1, b + NU)


def laid_out(x, c, ctx, c_ctx, ada_w, ada_b, post_ln_gain, post_ln_bias, even_w_in, even_q_gain, even_k_gain,
             even_f_gain, even_w_fmix, even_w_out, odd_w_in, odd_gate_bias, odd_w_out):
    a = {}
    a["x"] = np.concatenate([ctx[0], x[0]], 0)
    a["c_cols"] = np.stack([c[0].reshape(KD, P).T, c_ctx.reshape(KD, P).T], -1)
    a["ada_w"] = ada_w
    a["ada_b"] = ada_b
    a["ada_b_cols"] = ada_b[:, :2 * D].reshape(2, 16, P).transpose(2, 0, 1)
    a["post_gain"], a["post_bias"] = post_ln_gain, post_ln_bias
    w = even_w_in[0]
    q, ga, k, v, u, gb = np.split(w, np.cumsum([QW, QW, KVW, KVW, FW])[:5], axis=1)
    a["w0"] = np.concatenate([q, k, v, u, ga, gb], 1)
    a["qk_gain"] = np.concatenate([even_q_gain] * NQ + [even_k_gain] * NKV, 1)
    a["f_gain"] = even_f_gain.reshape(1, FW)
    mix = np.zeros((2, P, P), even_w_fmix.dtype)
    for g in range(4):
        o = (g % 2) * HD
        mix[g // 2, o:o + HD, o:o + HD] = even_w_fmix[0, g]
    a["fmix"] = mix
    a["w_out0"], a["w_out1"] = even_w_out[0], odd_w_out[0]
    w = odd_w_in[0]
    a["w1"] = np.concatenate([w[:, D:3 * D], w[:, 0:D], w[:, 3 * D:5 * D]], 1)
    wg = np.zeros((D, P), w.dtype)
    gb = np.zeros((P, 1), odd_gate_bias.dtype)
    for kind, row in ((0, 0), (1, 64), (2, 32), (3, 96)):
        wg[:, row:row + MH] = w[:, 5 * D + kind * MH:5 * D + (kind + 1) * MH]
        gb[row:row + MH, 0] = odd_gate_bias[0, kind * MH:(kind + 1) * MH]
    a["w_gate"], a["gate_bias"] = wg, gb
    return {n: np.ascontiguousarray(np.asarray(v)) for n, v in a.items()}


def tables():
    t = {"ident": np.eye(P)}
    t["fold"] = np.concatenate([np.concatenate([np.eye(HD)] * 2), np.zeros((P, P - HD))], 1)
    inv = 10000.0 ** -(np.arange(16, dtype=np.float32) / np.float32(16))
    inv = inv.astype(np.float32)
    n = np.arange(SEQ)
    ang = np.concatenate([(n // GRID_W).astype(np.float32)[:, None] * inv, (n % GRID_W).astype(np.float32)[:, None] * inv], 1)
    rope = np.zeros((T, 2, 32))
    rope[:CTX, 0] = 1.0
    rope[CTX:, 0], rope[CTX:, 1] = np.cos(ang.astype(np.float64)), np.sin(ang.astype(np.float64))
    t["rope"] = rope
    for name, length in (("dft_lat", SEQ), ("dft_ctx", CTX)):
        R = length // P
        p, r, mm = np.arange(P)[:, None, None], np.arange(R)[None, :, None], np.arange(P)[None, None, :]
        ang = 2 * np.pi * ((p * (R * mm + r)) % length) / length
        t[name] = np.stack([np.cos(ang), np.sin(ang)], 1) / np.sqrt(length * HD)
    j = np.arange(HD)
    ang = 2 * np.pi * (np.outer(j, j) % HD) / HD
    t["dft_head"] = np.stack([np.kron(np.eye(2), np.cos(ang)), np.kron(np.eye(2), -np.sin(ang))])
    s, q = np.arange(P)[:, None], np.arange(P)[None, :]
    t["mask"] = np.stack([np.where(s <= q, 0.0, MASKED), np.where(s >= q, 0.0, MASKED)])
    sel = np.zeros((P, 2 * MH, P))
    for d in range(2):
        for h in range(MH):
            sel[DIR_ROW[d] + h, d * MH + h] = 1.0
    t["sel"] = sel
    return {k: np.ascontiguousarray(v.astype(np.float32)) for k, v in t.items()}


def program(nc, a, out):
    m = Memory(nc)
    dram = lambda name, shape: nc.dram_tensor(name, list(shape), F32, kind="Internal").ap()
    s = {
        "gates": dram("s_gates", (3, P, D)),
        "proj0": dram("s_proj0", (T, W0_COLS)),
        "un": dram("s_un", (T, FW)),
        "q": dram("s_q", (NQ, NT, P, P)),
        "attn": dram("s_attn", (T, QW)),
        "four": dram("s_four", (T, FW)),
        "x1": dram("s_x1", (T, D)),
        "proj1": dram("s_proj1", (T, W1_COLS)),
        "h": dram("s_h", (2, SEQ, D)),
    }
    keep = {}
    for name, shape in (("mod", [P, 2, 2, NT, KD]), ("ident", [P, P])):
        keep[name] = m.all.enter_context(nc.sbuf_tensor("keep_" + name, shape, F32))
    setup = m.sem("ident_ld")
    with nc.Block() as block:

        @block.sync
        def _(sp):
            sp.dma_start(keep["ident"][:], a["ident"]).then_inc(setup, 16)
            sp.wait_ge(setup, 16)

    modulation(nc, m, a, s, keep)
    projections(nc, m, a, s, keep, 0, None)

    kres, vres = m.sb("kres", [P, 2 * NKV, T], F32R), m.sb("vres", [P, NT, NKV, P], F32R)
    attention_stack, m.stack = m.stack, ExitStack()
    heads(nc, m, a, s, keep, kres, vres)
    m.end()
    attention(nc, m, a, s, keep, kres, vres, "ac_", 0, CT, CT)
    m.end()
    attention(nc, m, a, s, keep, kres, vres, "al_", CT, LT, NT)
    m.end()
    attention_stack.close()
    out_weights = OutWeights(nc, m, 0, a["w_out0"])
    weights_stack, m.stack = m.stack, ExitStack()
    fourier(nc, m, a, s, keep, out_weights)
    m.end()
    mixer_out(nc, m, a, s, keep, 0, s["x1"], out_weights)
    weights_stack.close()

    graw = m.sb("graw", [P, T])
    gates_stack, m.stack = m.stack, ExitStack()
    projections(nc, m, a, s, keep, 1, graw)
    out_weights = OutWeights(nc, m, 1, a["w_out1"])
    weights_stack, m.stack = m.stack, ExitStack()
    mrow, cols, dec = m.sb("mrow", [P, T]), m.sb("cols", [P, NT, 2, 4, MH]), m.sb("dec", [P, 2 * MH, NT])
    scan_stack, m.stack = m.stack, ExitStack()
    gate_rows(nc, m, a, keep, graw, mrow, cols, dec)
    m.end()
    mlstm(nc, m, a, s, keep, mrow, cols, dec, out_weights)
    m.end()
    scan_stack.close()
    mixer_out(nc, m, a, s, keep, 1, out[0], out_weights)
    weights_stack.close()
    gates_stack.close()
    m.all.close()


def kernel(**inputs):
    from concourse import bacc
    from concourse.bass_utils import run_bass_kernel_spmd

    arrays = {**laid_out(**inputs), **tables()}
    nc = bacc.Bacc("TRN2", target_bir_lowering=False, num_devices=1)
    feed = {f"in_{n}": v for n, v in arrays.items()}
    aps = {n: nc.dram_tensor(f"in_{n}", v.shape, mybir.dt.from_np(v.dtype), kind="ExternalInput").ap() for n, v in arrays.items()}
    out = nc.dram_tensor("out_0", (1, SEQ, D), F32, kind="ExternalOutput").ap()
    program(nc, aps, out)
    r = run_bass_kernel_spmd(nc, [feed], core_ids=[0])
    return r.results[0]["out_0"]
```
